# Optimizing a Trainium2 kernel written in Bass

```python
import jax, jax.numpy as jnp
from jax import lax
import numpy as np

D_MODEL = 1024
BATCH = 1
SEQ = 1024
DEPTH = 1
DEC_BATCH = 8
DEC_SEQ = 16
PAST_LEN = 512

CHUNK = 64
Q_BLOCK = 128
EPS = 1e-6
ROPE_BASE = 10000.0

MLA_HEADS = 8
MLA_NOPE = 64
MLA_ROPE = 32
MLA_V = 64
MLA_Q_LORA = 256
MLA_KV_LORA = 128
MLA_SCALE = (MLA_NOPE + MLA_ROPE) ** -0.5
RET_HEADS = 4
RET_DK = 64
RET_DV = 64
RET_SCALE = RET_DK ** -0.5
SB_HEADS = 4
SB_HD = 64
SB_SCALE = SB_HD ** -0.5
MEM_TOKENS = 256
MEM_HEADS = 4
MEM_HD = 128
MEM_SCALE = MEM_HD ** -0.5
D_FF = 2816
CONV_W = 3

MLA_WIDTH = MLA_HEADS * MLA_V
RET_WIDTH = RET_HEADS * RET_DV
SB_WIDTH = SB_HEADS * SB_HD
MIX_WIDTH = MLA_WIDTH + RET_WIDTH + SB_WIDTH
IN_SIZES = (MLA_Q_LORA, MLA_KV_LORA, MLA_ROPE, RET_HEADS * RET_DK, RET_HEADS * RET_DK, RET_WIDTH, RET_WIDTH, SB_WIDTH, SB_WIDTH, SB_WIDTH)
IN_WIDTH = sum(IN_SIZES)
IN_SPLIT_POINTS = tuple(int(c) for c in np.cumsum(IN_SIZES)[:-1])

kernel_name = 'hybrid_mla_retention_stickbreak_streaming_step'

def rmsnorm(x, g):
    xf = x.astype(jnp.float32)
    y = xf * lax.rsqrt(jnp.mean(xf * xf, axis=-1, keepdims=True) + EPS)
    return (y * g.astype(jnp.float32)).astype(x.dtype)

def rope(x, pos):
    d = x.shape[-1]
    inv = ROPE_BASE ** (-jnp.arange(0, d, 2, dtype=jnp.float32) / d)
    ang = pos.astype(jnp.float32)[:, None] * inv[None, :]
    cos = jnp.cos(ang)[:, None, :]
    sin = jnp.sin(ang)[:, None, :]
    xf = x.astype(jnp.float32)
    x1, x2 = xf[..., : d // 2], xf[..., d // 2:]
    return jnp.concatenate([x1 * cos - x2 * sin, x1 * sin + x2 * cos], axis=-1).astype(x.dtype)

def head_norm(o, g):
    of = o.astype(jnp.float32)
    mu = jnp.mean(of, axis=-1, keepdims=True)
    var = jnp.mean(jnp.square(of - mu), axis=-1, keepdims=True)
    y = ((of - mu) * lax.rsqrt(var + EPS)).reshape(o.shape[0], o.shape[1], -1)
    return y * g.astype(jnp.float32)

def sweep_queries(attend, qs, q_pos):
    T = q_pos.shape[0]
    if T <= Q_BLOCK:
        return attend(*qs, q_pos)
    nb = T // Q_BLOCK
    blocks = tuple(jnp.moveaxis(a.reshape(a.shape[0], nb, Q_BLOCK, *a.shape[2:]), 1, 0) for a in qs)
    out = lax.map(lambda blk: attend(*blk[:-1], blk[-1]), blocks + (q_pos.reshape(nb, Q_BLOCK),))
    out = jnp.moveaxis(out, 0, 1)
    return out.reshape(out.shape[0], T, *out.shape[3:])

def mla_attend(q_nope, q_pe, k_nope, k_pe, v, q_pos, k_pos):
    s = (jnp.einsum('bqhd,bkhd->bhqk', q_nope, k_nope).astype(jnp.float32)
         + jnp.einsum('bqhr,bkr->bhqk', q_pe, k_pe).astype(jnp.float32)) * MLA_SCALE
    visible = (k_pos[None, :] // CHUNK) <= (q_pos[:, None] // CHUNK)
    s = jnp.where(visible[None, None], s, -jnp.inf)
    p = jax.nn.softmax(s, axis=-1).astype(v.dtype)
    return jnp.einsum('bhqk,bkhd->bqhd', p, v)

def stick_breaking_attend(q, k, v, q_pos, k_pos):
    z = jnp.einsum('bqhd,bkhd->bhqk', q, k).astype(jnp.float32) * SB_SCALE
    before = (k_pos[None, :] < q_pos[:, None])[None, None]
    log_beta = jax.nn.log_sigmoid(z)
    log_keep = jnp.where(before, jax.nn.log_sigmoid(-z), 0.0)
    between = lax.cumsum(log_keep, axis=3, reverse=True) - log_keep
    a = jnp.where(before, jnp.exp(log_beta + between), 0.0)
    return jnp.einsum('bhqk,bkhd->bqhd', a.astype(v.dtype), v)

def ret_log_gamma():
    return jnp.log(1.0 - 2.0 ** (-5.0 - jnp.arange(RET_HEADS, dtype=jnp.float32)))

def retention_chunkwise(q, k, v, log_gamma, s0):
    L = q.shape[2]
    qf, kf, vf = q.astype(jnp.float32), k.astype(jnp.float32), v.astype(jnp.float32)
    idx = jnp.arange(L, dtype=jnp.float32)
    diff = idx[:, None] - idx[None, :]
    decay_mask = jnp.where(diff[None] >= 0, jnp.exp(jnp.maximum(diff, 0.0)[None] * log_gamma[:, None, None]), 0.0)
    scores = jnp.einsum('bclhd,bcshd->bchls', qf, kf) * decay_mask[None, None]
    o_inner = jnp.einsum('bchls,bcshe->bclhe', scores, vf)
    decay_k = jnp.exp((L - 1.0 - idx)[:, None] * log_gamma[None, :])
    kv_chunk = jnp.einsum('bclhd,lh,bclhe->bchde', kf, decay_k, vf)
    chunk_decay = jnp.exp(L * log_gamma)[None, :, None, None]

    def step(s, kv_c):
        return chunk_decay * s + kv_c, s

    s_fin, s_prev = lax.scan(step, s0, jnp.moveaxis(kv_chunk, 1, 0))
    s_prev = jnp.moveaxis(s_prev, 0, 1)
    decay_q = jnp.exp((idx + 1.0)[:, None] * log_gamma[None, :])
    o_cross = jnp.einsum('bclhd,lh,bchde->bclhe', qf, decay_q, s_prev)
    return o_inner + o_cross, s_fin

def memory_kv(mem, g, w_k, w_v):
    m = rmsnorm(mem, g)
    B, M, _ = m.shape
    return (m @ w_k).reshape(B, M, MEM_HEADS, MEM_HD), (m @ w_v).reshape(B, M, MEM_HEADS, MEM_HD)

def memory_attend(x, mem_k, mem_v, g, w_q, w_o):
    B, T, _ = x.shape
    q = (rmsnorm(x, g) @ w_q).reshape(B, T, MEM_HEADS, MEM_HD)
    s = jnp.einsum('bqhd,bkhd->bhqk', q, mem_k.astype(q.dtype)).astype(jnp.float32) * MEM_SCALE
    p = jax.nn.softmax(s, axis=-1).astype(x.dtype)
    o = jnp.einsum('bhqk,bkhd->bqhd', p, mem_v.astype(x.dtype)).reshape(B, T, MEM_HEADS * MEM_HD)
    return o @ w_o

def conv_ffn(x, conv_prev, g, w_up, w_conv, b_conv, w_down):
    T = x.shape[1]
    u = rmsnorm(x, g) @ w_up
    ext = jnp.concatenate([conv_prev.astype(u.dtype), u], axis=1)
    c = b_conv
    for j in range(CONV_W):
        c = c + ext[:, j:j + T] * w_conv[j]
    a, b = jnp.split(c, 2, axis=-1)
    return (jax.nn.silu(a) * b) @ w_down, ext[:, T:]

def trunk_layer(x, pos, past, mem_k, mem_v, p):
    B, T, _ = x.shape
    h = rmsnorm(x, p['g_mix'])
    z = h @ p['w_in']
    cq, ckv, kpe, rq, rk, rv, rg, sq, sk, sv = jnp.split(z, IN_SPLIT_POINTS, axis=-1)
    q = (rmsnorm(cq, p['g_q_lora']) @ p['w_q_up']).reshape(B, T, MLA_HEADS, MLA_NOPE + MLA_ROPE)
    q_nope = q[..., :MLA_NOPE]
    q_pe = rope(q[..., MLA_NOPE:], pos)
    ckv = rmsnorm(ckv, p['g_kv_lora'])
    kpe = rope(kpe[:, :, None, :], pos)[:, :, 0, :]
    rq = rope(rq.reshape(B, T, RET_HEADS, RET_DK), pos)
    rk = rope(rk.reshape(B, T, RET_HEADS, RET_DK), pos) * RET_SCALE
    rv = rv.reshape(B, T, RET_HEADS, RET_DV)
    sq = sq.reshape(B, T, SB_HEADS, SB_HD)
    sk = sk.reshape(B, T, SB_HEADS, SB_HD)
    sv = sv.reshape(B, T, SB_HEADS, SB_HD)
    if past is None:
        ckv_all, kpe_all, sk_all, sv_all = ckv, kpe, sk, sv
        s0 = jnp.zeros((B, RET_HEADS, RET_DK, RET_DV), jnp.float32)
        conv0 = jnp.zeros((B, CONV_W - 1, 2 * D_FF), x.dtype)
        n_chunks = T // CHUNK
    else:
        ckv_c, kpe_c, s0, sk_c, sv_c, conv0 = past
        ckv_all = jnp.concatenate([ckv_c.astype(x.dtype), ckv], axis=1)
        kpe_all = jnp.concatenate([kpe_c.astype(x.dtype), kpe], axis=1)
        sk_all = jnp.concatenate([sk_c.astype(x.dtype), sk], axis=1)
        sv_all = jnp.concatenate([sv_c.astype(x.dtype), sv], axis=1)
        n_chunks = 1
    k_pos = jnp.arange(ckv_all.shape[1])
    kv = (ckv_all @ p['w_kv_up']).reshape(B, -1, MLA_HEADS, MLA_NOPE + MLA_V)
    k_nope, v_mla = kv[..., :MLA_NOPE], kv[..., MLA_NOPE:]
    o_mla = sweep_queries(lambda a, b, qp: mla_attend(a, b, k_nope, kpe_all, v_mla, qp, k_pos), (q_nope, q_pe), pos)
    L = T // n_chunks

    def chunked(a):
        return a.reshape(B, n_chunks, L, *a.shape[2:])

    o_ret, s_new = retention_chunkwise(chunked(rq), chunked(rk), chunked(rv), ret_log_gamma(), s0.astype(jnp.float32))
    o_sb = sweep_queries(lambda a, qp: stick_breaking_attend(a, sk_all, sv_all, qp, k_pos), (sq,), pos)
    ret_y = head_norm(o_ret.reshape(B, T, RET_HEADS, RET_DV), p['g_ret_norm']).astype(x.dtype) * jax.nn.silu(rg)
    mixed = jnp.concatenate([o_mla.reshape(B, T, MLA_WIDTH), ret_y, o_sb.reshape(B, T, SB_WIDTH)], axis=-1)
    x = x + mixed @ p['w_out']
    x = x + memory_attend(x, mem_k, mem_v, p['g_mem_q'], p['w_mem_q'], p['w_mem_o'])
    y, conv_new = conv_ffn(x, conv0, p['g_ffn'], p['w_ffn_up'], p['w_ffn_conv'], p['b_ffn_conv'], p['w_ffn_down'])
    x = x + y
    return x, (ckv, kpe, s_new.astype(x.dtype), sk, sv, conv_new)

def setup_inputs(seed: int = 0) -> dict:
    key = jax.random.key(seed)
    ks = iter(jax.random.split(key, 40))

    def nrm(shape, scale=1.0):
        return jax.random.normal(next(ks), shape, jnp.float32) * scale

    def gain(shape):
        return 1.0 + nrm(shape, 0.02)

    f2 = 2 * D_FF
    mem_w = MEM_HEADS * MEM_HD
    return {
        'x_prompt': nrm((BATCH, SEQ, D_MODEL)),
        'x_sample': nrm((DEC_BATCH, DEC_SEQ, D_MODEL)),
        'cache_mla_ckv': nrm((DEPTH, DEC_BATCH, PAST_LEN, MLA_KV_LORA)),
        'cache_mla_kpe': nrm((DEPTH, DEC_BATCH, PAST_LEN, MLA_ROPE)),
        'state_ret': nrm((DEPTH, DEC_BATCH, RET_HEADS, RET_DK, RET_DV), 0.1),
        'cache_sb_k': nrm((DEPTH, DEC_BATCH, PAST_LEN, SB_HEADS, SB_HD)),
        'cache_sb_v': nrm((DEPTH, DEC_BATCH, PAST_LEN, SB_HEADS, SB_HD)),
        'cache_mem_k': nrm((DEPTH, DEC_BATCH, MEM_TOKENS, MEM_HEADS, MEM_HD)),
        'cache_mem_v': nrm((DEPTH, DEC_BATCH, MEM_TOKENS, MEM_HEADS, MEM_HD)),
        'state_ffn_conv': nrm((DEPTH, DEC_BATCH, CONV_W - 1, f2)),
        'mem_prompt': nrm((BATCH, MEM_TOKENS, D_MODEL)),
        'g_mix': gain((DEPTH, D_MODEL)),
        'w_in': nrm((DEPTH, D_MODEL, IN_WIDTH), D_MODEL ** -0.5),
        'g_q_lora': gain((DEPTH, MLA_Q_LORA)),
        'w_q_up': nrm((DEPTH, MLA_Q_LORA, MLA_HEADS * (MLA_NOPE + MLA_ROPE)), MLA_Q_LORA ** -0.5),
        'g_kv_lora': gain((DEPTH, MLA_KV_LORA)),
        'w_kv_up': nrm((DEPTH, MLA_KV_LORA, MLA_HEADS * (MLA_NOPE + MLA_V)), MLA_KV_LORA ** -0.5),
        'g_ret_norm': gain((DEPTH, RET_WIDTH)),
        'w_out': nrm((DEPTH, MIX_WIDTH, D_MODEL), MIX_WIDTH ** -0.5),
        'g_mem_q': gain((DEPTH, D_MODEL)),
        'g_mem_kv': gain((DEPTH, D_MODEL)),
        'w_mem_q': nrm((DEPTH, D_MODEL, mem_w), D_MODEL ** -0.5),
        'w_mem_k': nrm((DEPTH, D_MODEL, mem_w), D_MODEL ** -0.5),
        'w_mem_v': nrm((DEPTH, D_MODEL, mem_w), D_MODEL ** -0.5),
        'w_mem_o': nrm((DEPTH, mem_w, D_MODEL), mem_w ** -0.5),
        'g_ffn': gain((DEPTH, D_MODEL)),
        'w_ffn_up': nrm((DEPTH, D_MODEL, f2), D_MODEL ** -0.5),
        'w_ffn_conv': nrm((DEPTH, CONV_W, f2), CONV_W ** -0.5),
        'b_ffn_conv': nrm((DEPTH, f2), 0.01),
        'w_ffn_down': nrm((DEPTH, D_FF, D_MODEL), D_FF ** -0.5),
        'g_final': gain((D_MODEL,)),
    }

def reference(x_prompt, x_sample, cache_mla_ckv, cache_mla_kpe, state_ret, cache_sb_k, cache_sb_v,
              cache_mem_k, cache_mem_v, state_ffn_conv, mem_prompt,
              g_mix, w_in, g_q_lora, w_q_up, g_kv_lora, w_kv_up, g_ret_norm, w_out,
              g_mem_q, g_mem_kv, w_mem_q, w_mem_k, w_mem_v, w_mem_o,
              g_ffn, w_ffn_up, w_ffn_conv, b_ffn_conv, w_ffn_down, g_final):
    params = [dict(g_mix=g_mix[l], w_in=w_in[l], g_q_lora=g_q_lora[l], w_q_up=w_q_up[l],
                   g_kv_lora=g_kv_lora[l], w_kv_up=w_kv_up[l], g_ret_norm=g_ret_norm[l], w_out=w_out[l],
                   g_mem_q=g_mem_q[l], w_mem_q=w_mem_q[l], w_mem_o=w_mem_o[l],
                   g_ffn=g_ffn[l], w_ffn_up=w_ffn_up[l], w_ffn_conv=w_ffn_conv[l],
                   b_ffn_conv=b_ffn_conv[l], w_ffn_down=w_ffn_down[l]) for l in range(DEPTH)]

    xp = x_prompt
    pos_p = jnp.arange(xp.shape[1])
    p_states, p_mem_k, p_mem_v = [], [], []
    for l in range(DEPTH):
        mk, mv = memory_kv(mem_prompt, g_mem_kv[l], w_mem_k[l], w_mem_v[l])
        xp, st = trunk_layer(xp, pos_p, None, mk, mv, params[l])
        p_states.append(st)
        p_mem_k.append(mk)
        p_mem_v.append(mv)
    y_prompt = rmsnorm(xp, g_final)

    xs = x_sample
    past_len = cache_mla_ckv.shape[2]
    pos_s = past_len + jnp.arange(xs.shape[1])
    s_states = []
    for l in range(DEPTH):
        past = (cache_mla_ckv[l], cache_mla_kpe[l], state_ret[l], cache_sb_k[l], cache_sb_v[l], state_ffn_conv[l])
        xs, st = trunk_layer(xs, pos_s, past, cache_mem_k[l], cache_mem_v[l], params[l])
        s_states.append(st)
    y_sample = rmsnorm(xs, g_final)

    p_ckv, p_kpe, p_ret, p_sbk, p_sbv, p_conv = [jnp.stack(f) for f in zip(*p_states)]
    s_ckv, s_kpe, s_ret, s_sbk, s_sbv, s_conv = [jnp.stack(f) for f in zip(*s_states)]
    p_memk = jnp.stack(p_mem_k)
    p_memv = jnp.stack(p_mem_v)
    return (y_prompt, y_sample, p_ckv, p_kpe, p_ret, p_sbk, p_sbv, p_memk, p_memv, p_conv,
            s_ckv, s_kpe, s_ret, s_sbk, s_sbv, s_conv)


_drawn_inputs = setup_inputs


def setup_inputs(seed=0):
    import zlib

    import numpy as np

    out = dict(_drawn_inputs(seed))
    spreads = {}
    factors = {'g_q_lora': 8.0,
     'g_kv_lora': 2.812,
     'g_ret_norm': 8.0,
     'g_mem_q': 8.0,
     'g_mem_kv': 2.939,
     'g_ffn': 2.776,
     'b_ffn_conv': 8.0,
     'g_final': 2.756}
    for name, (base, spread) in spreads.items():
        noise = np.random.default_rng([zlib.crc32(name.encode()), seed]).standard_normal(out[name].shape)
        drawn = base * np.exp(spread * noise) if base else spread * noise
        out[name] = __import__('jax').numpy.asarray(drawn.astype(out[name].dtype))
    for name, factor in factors.items():
        out[name] = (out[name] * factor).astype(out[name].dtype)
    return out
```

```python
from contextlib import ExitStack

import numpy as np

import concourse.bass as bass
from concourse import mybir

F32 = mybir.dt.float32
F32R = mybir.dt.float32r
ALU = mybir.AluOpType
ACT = mybir.ActivationFunctionType
AX = mybir.AxisListType

P = 128
D = 1024
KB = D // P
TP = 1024
DB, DS = 8, 16
TS = DB * DS
T = TP + TS
CH = 384
NCH = T // CH
PAST = 512
MEM = 256
DFF = 2816
NFF = DFF // P
EPS = 1e-6
NEG = -1e30
QL, KVL, NOPE, ROPE, VD = 256, 128, 64, 32, 64
MH = 8
RH = 4
SH = 4
HD = 64
GH = 4
MLA_SCALE = (NOPE + ROPE) ** -0.5
MEM_SCALE = P ** -0.5
NTILE = TP // P
NT = T // P

Z_CQ, Z_CKV, Z_KPE, Z_RQ, Z_RK, Z_RG, Z_SQ, Z_SK, NZ = 0, 2, 3, 4, 6, 8, 10, 14, 18

W_MEM = 0
W_IN = W_MEM + 8
W_OUT = W_IN + NZ
W_MQ = W_OUT + KB
W_MO = W_MQ + GH
W_FFN = W_MO + 4
NGRP = NFF // 2
NW = W_FFN + 6 * NGRP

G_IN = 0
G_OUT = G_IN + NZ * NCH
G_MQ = G_OUT + KB * NCH
G_MO = G_MQ + GH * NCH
G_UP = G_MO + KB * NCH
UP_BEFORE = 2 * (NZ + KB + GH) + 5 * 4
EXT = 2 + TP + DB * (2 + DS)

CONSTS = (("g_mix", KB), ("g_mem_q", KB), ("g_mem_kv", KB), ("g_ffn", KB), ("g_final", KB),
          ("g_q", 2), ("g_kv", 1), ("g_ret", 2), ("decay128", 2), ("decay16", 2),
          ("b_conv", 2 * NFF), ("w_conv", 6 * NFF))
CONST_AT = {}
NCONST = 0
for _name, _n in CONSTS:
    CONST_AT[_name] = NCONST
    NCONST += _n

S_WIDTHS = (512, 512, 128)
S_AT = (0, 512, 1024)


def sum_chunks(first):
    return [(first + n, 6 + (first + n) % 2, S_AT[n], S_WIDTHS[n]) for n in range(3)]


Q_MEM, Q_X, Q_CQ, Q_CKV, Q_HEAD, Q_MQ, Q_FFN, Q_FINAL = 0, 1, 4, 7, 10, 22, 25, 28

NP = 4
N_LOOP = 3 * NTILE
KINDS = [(n % 3, n // 3) for n in range(N_LOOP)]


def n_groups(blocks):
    return (blocks + 3) // 4


G_BEFORE = [sum(n_groups(j + 1) for _, j in KINDS[:n]) for n in range(N_LOOP + 1)]
G_PASS = G_BEFORE[-1]
T_MLA_S = NP * N_LOOP
T_SB_S = T_MLA_S + DB
G_MLA_S = NP * G_PASS
G_SB_S = G_MLA_S + 2 * DB
G_SAMPLE_END = G_SB_S + 2 * (DB // 2)


def build(nc, io):
    ctx = ExitStack()
    with ctx:
        def sem(name):
            return ctx.enter_context(nc.semaphore(name))

        base = (nc.sbuf_base + 63) // 64 * 64
        top = nc.sbuf_top
        ctx.enter_context(nc.sbuf_tensor("slab", [P, (top - base - 64) // 4], F32))

        class Region:
            def __init__(self, at, size):
                self.at, self.end = at, at + size

            def __call__(self, name, shape, dt=F32):
                size = 4 * int(np.prod(shape[1:]))
                t = nc.alloc_sbuf_tensor_at(name, list(shape), dt, offset=self.at)
                self.at += (size + 31) // 32 * 32
                assert self.at <= self.end, (name, self.at - self.end)
                return t

        ROW = 4 * T
        off_w = base
        off_s = off_w + 24576
        off_a = off_s + 31552
        off_b = off_a + 2 * KB * ROW
        end_b = off_b + NZ * ROW
        assert end_b <= top, (end_b, top)

        r = Region(off_w, 24576)
        w_raw = r("w_raw", [P, 2, KB, P])
        w_hi = r("w_hi", [P, 2, KB, P], F32R)
        w_lo = r("w_lo", [P, 2, KB, P], F32R)

        r = Region(off_s, off_a - off_s)
        consts = r("consts", [P, NCONST])
        ident = r("ident", [P, P])
        ones = r("ones", [P, P])
        bd = r("bd", [P, P])
        eps = r("eps", [P, 1])
        zero = r("zero", [P, 1])
        at_mkv = r.at
        mkv = r("mkv", [P, 8, MEM])
        at_mv = r.at - 4 * 4 * MEM
        mem_v = r("mem_v", [P, 2, GH * P])
        at_rstd = r.at
        rstd = r("rstd", [P, T])
        at_square = r.at
        square = r("square", [P, T])
        sumsq = r("sumsq", [P, T])
        assert off_a - r.at >= 0

        r = Region(off_a, off_b - off_a)
        act_hi = r("act_hi", [P, KB, T], F32R)
        act_lo = r("act_lo", [P, KB, T], F32R)
        z = Region(off_b, NZ * ROW)("z", [P, NZ, T])
        x_in = Region(off_b + 10 * ROW, 8 * ROW)("x_in", [P, KB, T])
        r = Region(off_b, 10 * ROW)
        m_in = r("m_in", [P, KB, MEM])
        m_hi = r("m_hi", [P, KB, MEM], F32R)
        m_lo = r("m_lo", [P, KB, MEM], F32R)
        m_sq = r("m_sq", [P, KB, MEM])
        m_rstd = r("m_rstd", [P, MEM])

        r = Region(off_a, off_b - off_a)
        mixed = r("mixed", [P, KB, T])
        sv_tok = r("sv_tok", [P, NT, SH, HD])
        at_f1 = r.at
        rv_tok = r("rv_tok", [P, NT, RH, HD])
        kd_tok = r("kd_tok", [P, NT, RH, HD])
        ret_mask = r("ret_mask", [P, 2, 2, 2 * P])
        q_decay = r("q_decay", [P, 2, 2, P])
        k_decay = r("k_decay", [P, 2, RH, HD])
        r = Region(off_a, 4 * ROW)
        s0 = r("s0", [P, DB, 2, P])
        v_own = r("v_own", [P, 2, DB, P])
        own = r("own", [P, DB])
        r = Region(off_b + 16 * ROW, 2 * ROW)
        rope_cos = r("rope_cos", [P, T])
        rope_sin = r("rope_sin", [P, T])
        swap = square
        r = Region(at_square, 2 * ROW)
        kept = r("kept", [P, 2, 2, 2 * P])
        state = r("state", [P, 2, P])
        q_dec = r("q_dec", [P, 2, 2, P])

        r = Region(at_f1, off_b - at_f1)
        prob = r("prob", [P, 3, 1024])
        probT = r("probT", [P, 3, 512])
        soft = r("soft", [P, 1024])
        sv_pass = r("sv_pass", [P, NTILE, HD])
        neg_max = r("neg_max", [P, 4])
        row_sum = r("row_sum", [P, 4])
        before = r("before", [P, 2, P])
        r = Region(off_b + 4 * ROW, 6 * ROW)
        q_pass = r("q_pass", [P, 2, T])
        k_pass = r("k_pass", [P, 2, TP])
        rope_pe = r("rope_pe", [P, T])
        v_pass = r("v_pass", [P, NTILE, P])
        r = Region(at_square, 2 * ROW)
        sb_q = r("sb_q", [P, TP])
        log_term = r("log_term", [P, TP])
        q_abs = Region(at_rstd, ROW)("q_abs", [P, DB, MH, DS])
        w_pass = Region(at_mv, 4096)("w_pass", [P, 1024])
        rope_tmp = prob[64:96].rearrange("p a n -> p (a n)")[:, 0:2 * T].rearrange("p (a n) -> p a n", a=2)
        q_pe = z[64:96, Z_SQ, 0:DB * MH * DS].rearrange("p (b h t) -> p b h t", b=DB, h=MH)

        lat_at = off_b + 4 * ROW
        r = Region(lat_at, 6 * ROW)
        lat = r("lat", [P, 2, 3, PAST])
        o_lat = r("o_lat", [P, DB, MH, DS])
        w_v = r("w_v", [P, MH * VD])
        ckv_new = r("ckv_new", [P, KVL])
        cache_v0 = r("cache_v0", [P, 2, 4, SH * HD])
        cache_k0 = Region(off_b, 2 * ROW)("cache_k0", [P, 2, 2, PAST])
        r = Region(lat_at, 6 * ROW)
        cache_k1 = r("cache_k1", [P, 2, 2, PAST])
        cache_v1 = r("cache_v1", [P, 2, 4, SH * HD])
        cache_k, cache_v = (cache_k0, cache_k1), (cache_v0, cache_v1)
        r = Region(at_f1 + 4 * (3 * 1024 + 3 * 512 + 1024), 4 * NTILE * HD)
        own_band = r("own_band", [P, 15 * DS])
        keep_band = r("keep_band", [P, 14 * DS])
        hide_band = Region(at_f1 + 25664 + 64, 1024)("hide_band", [P, 14 * DS])
        r = Region(at_square, 2 * ROW)
        sb_pair = r("sb_pair", [P, 2, 2, 2, P])
        r = Region(at_square + 8192, 1024)
        sk_new = r("sk_new", [P, 2, TS])

        r = Region(off_b, NZ * ROW)
        mix_hi = r("mix_hi", [P, KB, T], F32R)
        mix_lo = r("mix_lo", [P, KB, T], F32R)
        x_blk = r("x_blk", [P, 2, T])
        at_x = off_b + 10 * ROW
        x = Region(at_x, KB * ROW)("x", [P, KB, T])
        qm = Region(at_x, KB * ROW)("qm", [P, GH, T])
        r = Region(off_b, 8 * ROW)
        om_hi = r("om_hi", [P, GH, T], F32R)
        om_lo = r("om_lo", [P, GH, T], F32R)
        r = Region(off_a, off_b - off_a)
        m_prob = r("m_prob", [P, 2, GH * MEM])
        m_probT = r("m_probT", [P, 4, 512])
        mk_c = r("mk_c", [P, 2, 2, GH, MEM])
        mv_c = r("mv_c", [P, 2, 2, 2, GH * P])
        qm_pair = r("qm_pair", [P, 2, 2, GH, P])
        m_max = r("m_max", [P, 2, GH])
        m_sum = r("m_sum", [P, 2, GH])

        r = Region(off_b, 10 * ROW)
        s_hi = r("s_hi", [P, 2, T], F32R)
        s_lo = r("s_lo", [P, 2, T], F32R)
        ext = r("ext", [P, 2, EXT])
        conv = r("conv", [P, 2, EXT])
        r = Region(at_mkv, 12288)
        conv0 = r("conv0", [P, 2 * NFF, 2 * DB])
        conv_new = r("conv_new", [P, 2 * NFF, 2 + 2 * DB])

        S = [ctx.enter_context(nc.psum_tensor(f"scores{i}", [P, 1024], F32)) for i in range(2)]
        bank = [S[i // 2][:, 512 * (i % 2):512 * (i % 2) + 512] for i in range(4)]
        bank += [ctx.enter_context(nc.psum_tensor(f"bank{i}", [P, 512], F32))[:] for i in range(4, 8)]

        def const(name, k=0, n=1, rows=slice(0, P)):
            return consts[rows, CONST_AT[name] + k:CONST_AT[name] + k + n]

        consts_in, m_loaded, rope_in, ret_in = sem("consts_in"), sem("m_loaded"), sem("rope_in"), sem("ret_in")
        x_loaded = [sem(f"x_loaded{i}") for i in range(4)]
        w_loaded = [sem(f"w_loaded{i}") for i in range(2)]
        stored_mkv, stored_skv, stored_ckv = sem("stored_mkv"), sem("stored_skv"), sem("stored_ckv")
        stored_state, stored_s0 = sem("stored_state"), sem("stored_s0")
        zero_set, w_rounded, w_split, w_used = sem("zero_set"), sem("w_rounded"), sem("w_split"), sem("w_used")
        g_done, g_evac = sem("g_done"), sem("g_evac")
        sum_ready, sum_used, rstd_ready = sem("sum_ready"), sem("sum_used"), sem("rstd_ready")
        setup_done = sem("setup_done")
        m_squared, m_gained, m_rounded, m_split = sem("m_squared"), sem("m_gained"), sem("m_rounded"), sem("m_split")
        mem_evac, memT_done, memv_ready = sem("mem_evac"), sem("memT_done"), sem("memv_ready")
        x_squared, x_rounded, x_summed, x_split = sem("x_squared"), sem("x_rounded"), sem("x_summed"), sem("x_split")
        lora_squared, lora_summed, lora_normed = sem("lora_squared"), sem("lora_summed"), sem("lora_normed")
        swapped, swap_used = sem("swapped"), sem("swap_used")
        dve_own, act_own = sem("dve_own"), sem("act_own")
        tokT_done, kd_ready, tok_ready = sem("tokT_done"), sem("kd_ready"), sem("tok_ready")
        ret_scores, ret_kept, ret_q, ret_o = sem("ret_scores"), sem("ret_kept"), sem("ret_q"), sem("ret_o")
        ret_o_evac, ret_kv, ret_state = sem("ret_o_evac"), sem("ret_kv"), sem("ret_state")
        v_own_ready, s0_new = sem("v_own_ready"), sem("s0_new")
        head_squared, gated, ret_done = sem("head_squared"), sem("gated"), sem("ret_done")

        w_pass_in, attn_in, kpe_rotated, kpe_swapped, kpe_ready = (
            sem("w_pass_in"), sem("attn_in"), sem("kpe_rotated"), sem("kpe_swapped"), sem("kpe_ready"))
        stored_kpe = sem("stored_kpe")
        pass_done, q_evac, kv_evac, q_swapped, q_ready, sb_staged = (
            sem("pass_done"), sem("q_evac"), sem("kv_evac"), sem("q_swapped"), sem("q_ready"), sem("sb_staged"))
        s_ready, row_max, exp_done, p_norm = sem("s_ready"), sem("row_max"), sem("exp_done"), sem("p_norm")
        sb_log, sb_arg, sb_p = sem("sb_log"), sem("sb_arg"), sem("sb_p")
        pt_done, pt_copied, pv_done, o_evac = sem("pt_done"), sem("pt_copied"), sem("pv_done"), sem("o_evac")

        sample_in, lat_in = sem("sample_in"), [sem("lat_in0"), sem("lat_in1")]
        cache_in = [sem("cache_in0"), sem("cache_in1")]
        new_done, new_ready, o_heads, o_sample = sem("new_done"), sem("new_ready"), sem("o_heads"), sem("o_sample")
        sb_pair_ready, sk_new_ready = sem("sb_pair_ready"), sem("sk_new_ready")
        mix_rounded, mix_split = sem("mix_rounded"), sem("mix_split")
        xb_in, xb_out = [sem("xb_in0"), sem("xb_in1")], [sem("xb_out0"), sem("xb_out1")]
        ms_ready, m_row_max, m_exp, m_norm, mt_done, mt_copied, m_pv, om_rounded, om_split = (
            sem(n) for n in ("ms_ready", "m_row_max", "m_exp", "m_norm", "mt_done", "mt_copied", "m_pv",
                             "om_rounded", "om_split"))
        m_cache_in, qm_zero, qm_pair_ready, x_in_again = ([sem("m_cache_in0"), sem("m_cache_in1")], sem("qm_zero"),
                                                          sem("qm_pair_ready"), sem("x_in_again"))

        conv0_in, ext_zero, tap0_done, conv_done, silu_done, s_product, s_rounded, s_split, d_done, d_evac, y_ready = (
            sem(n) for n in ("conv0_in", "ext_zero", "tap0_done", "conv_done", "silu_done", "s_product", "s_rounded",
                             "s_split", "d_done", "d_evac", "y_ready"))
        stored_conv, stored_y = sem("stored_conv"), sem("stored_y")

        def sample_rows(t, first, n):
            return t[:, TP + 2:EXT].rearrange("p (b r) -> p b r", b=DB)[:, :, first:first + n]

        def conv_tap(blk, tap):
            return consts[:, bass.ds(3 * blk + (CONST_AT["w_conv"] + tap), 1)]

        def conv_bias(blk):
            return consts[:, bass.ds(blk + CONST_AT["b_conv"], 1)]

        def chunk_done(eng, slot, before, c):
            if c < NCH - 1:
                eng.wait_ge(g_done, before + c + 1)
            else:
                eng.wait_ge(w_used, slot + 1)

        def halves(block_of_z):
            return [(block_of_z, slice(0, 64)), (block_of_z, slice(64, P))]

        def frames(c):
            return slice(CH * c, CH * c + CH)

        def tile(c):
            return slice(P * c, P * c + P)

        class Own:
            def __init__(self, eng, s):
                self.eng, self.s, self.n, self.base = eng, s, 0, 0

            def __call__(self, ins):
                ins.then_inc(self.s, 1)
                self.n += 1

            def settle(self):
                self.eng.wait_ge(self.s, self.base + self.n)

            def enter(self, i, per):
                self.base, self.before, self.n, self.per = self.n + per * i, self.n, 0, per

            def leave(self, rounds):
                assert self.n == self.per, self.n
                self.base, self.n = 0, self.before + rounds * self.per

        block = ctx.enter_context(nc.Block())

        @block.sync
        def _(sp):
            sp.dma_start(m_in[:], io["mT"]).then_inc(m_loaded, 16)
            sp.dma_start(consts[:], io["consts"]).then_inc(consts_in, 16)
            sp.dma_start(ident[:], io["ident"]).then_inc(consts_in, 16)
            sp.dma_start(bd[:], io["bd"]).then_inc(consts_in, 16)
            for k in range(2):
                sp.dma_start(w_raw[:, k], io["wstream"][k]).then_inc(w_loaded[k], 16)
            for i in range(4):
                sp.dma_start(x_in[:, 2 * i:2 * i + 2], io["xT"][:, 2 * i:2 * i + 2]).then_inc(x_loaded[i], 16)

            def stream(first, last):
                with sp.Fori(first // 2, last // 2) as i:
                    for k in range(2):
                        sp.wait_ge(w_split, 2 * i + k - 1)
                        src = io["wstream"][bass.ds(2 * i + k, 1)].rearrange("a p n -> (a p) n")
                        sp.dma_start(w_raw[:, k], src).then_inc(w_loaded[k], 16)

            stream(2, W_IN)
            sp.wait_ge(x_split, KB)
            sp.wait_ge(x_summed, KB)
            sp.dma_start(rope_cos[:], io["rope_ret"][0]).then_inc(rope_in, 16)
            sp.dma_start(rope_sin[:], io["rope_ret"][1]).then_inc(rope_in, 16)
            stream(W_IN, W_OUT)
            sp.wait_ge(mem_evac, 8)
            sp.dma_start(io["o_mkv"], mkv[:]).then_inc(stored_mkv, 16)
            sp.wait_ge(w_used, W_OUT)
            for dst, name in ((ret_mask, "ret_mask"), (q_decay, "q_decay"), (k_decay, "k_decay"), (s0, "s0"),
                              (own, "own")):
                sp.dma_start(dst[:], io[name]).then_inc(ret_in, 16)
            sp.wait_ge(g_evac, NZ * NCH)
            sp.dma_start(io["o_skv"], z[:, Z_SQ:NZ]).then_inc(stored_skv, 16)
            sp.wait_ge(lora_normed, 3)
            sp.dma_start(io["o_ckv"], z[:, Z_CKV]).then_inc(stored_ckv, 16)
            sp.wait_ge(ret_state, NTILE)
            sp.dma_start(io["o_state"], state[:]).then_inc(stored_state, 16)
            sp.wait_ge(s0_new, 8)
            sp.dma_start(io["o_s0"], s0[:]).then_inc(stored_s0, 16)
            sp.wait_ge(ret_done, 4)
            sp.wait_ge(stored_mkv, 16)
            sp.dma_start(rope_pe[:], io["rope_pe"]).then_inc(attn_in, 16)
            sp.dma_start(before[:], io["before"]).then_inc(attn_in, 16)
            stream(W_OUT, W_OUT + 4)
            sp.dma_start(w_pass[:], io["w_pass"][0]).then_inc(w_pass_in, 16)
            with sp.Fori(1, NP) as i:
                sp.wait_ge(pass_done, 12 * i)
                sp.dma_start(w_pass[:], io["w_pass"][bass.ds(i, 1)].rearrange("a p n -> (a p) n")).then_inc(w_pass_in, 16)
            sp.wait_ge(kpe_ready, 1)
            sp.dma_start(io["o_kpe"], z[64:96, Z_KPE]).then_inc(stored_kpe, 16)
            sp.wait_ge(pv_done, G_MLA_S)
            sp.wait_ge(o_evac, T_MLA_S)
            for dst, name in ((own_band, "own_band"), (keep_band, "keep_band"), (hide_band, "hide_band"), (w_v, "w_v")):
                sp.dma_start(dst[:], io[name]).then_inc(sample_in, 16)

            def load_cache(p):
                sp.dma_start(cache_k[p % 2][:], io["cache_k"][p]).then_inc(cache_in[p % 2], 16)
                sp.dma_start(cache_v[p % 2][:], io["cache_v"][p]).then_inc(cache_in[p % 2], 16)

            for b in range(DB):
                if b >= 2:
                    sp.wait_ge(pv_done, G_MLA_S + 2 * (b - 1))
                sp.dma_start(lat[:, b % 2, 0], io["lat"][b, 0]).then_inc(lat_in[b % 2], 16)
                sp.dma_start(lat[64:96, b % 2, 1], io["kpe_c"][b]).then_inc(lat_in[b % 2], 16)
                sp.dma_start(lat[:, b % 2, 2], io["lat"][b, 1]).then_inc(lat_in[b % 2], 16)
                if b == 1:
                    load_cache(0)
            sp.wait_ge(o_heads, 1)
            load_cache(1)
            for p in range(2, DB // 2):
                sp.wait_ge(pv_done, G_SB_S + 2 * (p - 1))
                load_cache(p)
            stream(W_OUT + 4, W_FFN)
            sp.wait_ge(w_used, W_MO)

            def load_memory(p):
                sp.dma_start(mk_c[:, p % 2], io["mk_c"][p]).then_inc(m_cache_in[p % 2], 16)
                sp.dma_start(mv_c[:, p % 2], io["mv_c"][p]).then_inc(m_cache_in[p % 2], 16)

            load_memory(0)
            load_memory(1)
            for p in range(2, DB // 2):
                sp.wait_ge(m_pv, NTILE + p - 1)
                load_memory(p)
            sp.wait_ge(m_pv, NTILE + DB // 2)
            for k in range(2):
                sp.wait_ge(xb_out[k], 16 * KB // 2)
            sp.dma_start(x[:], io["x_mid"]).then_inc(x_in_again, 16)
            sp.dma_start(conv0[:], io["conv0"]).then_inc(conv0_in, 16)
            stream(W_FFN, NW)
            sp.wait_ge(tap0_done, 2 * NFF)
            sp.dma_start(io["o_conv"], conv_new[:]).then_inc(stored_conv, 16)
            for m in range(KB):
                sp.wait_ge(y_ready, m + 1)
                sp.dma_start(io["o_y"][:, m], x[:, m]).then_inc(stored_y, 16)
            for stored, n in ((stored_mkv, 1), (stored_skv, 1), (stored_ckv, 1), (stored_state, 1), (stored_s0, 1),
                              (stored_kpe, 1), (stored_conv, 1), (stored_y, KB)):
                sp.wait_ge(stored, 16 * n)

        @block.gpsimd
        def _(pool):
            pool.memset(zero[:], 0.0).then_inc(zero_set, 1)
            pool.wait_ge(zero_set, 1)

            def split(k, rounded):
                pool.tensor_tensor(w_hi[:, k], w_raw[:, k], zero[:].unsqueeze(2).to_broadcast([P, KB, P]),
                                   ALU.add).then_inc(w_rounded, 1)
                pool.wait_ge(w_rounded, rounded)
                pool.tensor_tensor(w_lo[:, k], w_raw[:, k], w_hi[:, k].bitcast(F32),
                                   ALU.subtract).then_inc(w_split, 1)

            for k in range(2):
                pool.wait_ge(w_loaded[k], 16)
                split(k, k + 1)
            with pool.Fori(1, NW // 2) as i:
                for k in range(2):
                    pool.wait_ge(w_loaded[k], 16 * i + 16)
                    pool.wait_ge(w_used, 2 * i + k - 1)
                    split(k, 2 * i + k + 1)

        @block.scalar
        def _(act):
            own_a = Own(act, act_own)

            def roots(q, width, dst, n_frames=None):
                for n, b, at, w in sum_chunks(q) if n_frames is None else [(q, 6 + q % 2, 0, n_frames)]:
                    act.wait_ge(sum_ready, n + 1)
                    act.activation(dst[:, at:at + w], bank[b][:, 0:w], ACT.Sqrt, bias=eps[:],
                                   scale=1.0 / width).then_inc(sum_used, 1)

            act.wait_ge(m_loaded, 16)
            act.activation(m_sq[:], m_in[:], ACT.Square).then_inc(m_squared, 1)
            act.wait_ge(m_gained, 1)
            act.activation(m_hi[:], m_in[:], ACT.Copy).then_inc(m_rounded, 1)
            act.wait_ge(setup_done, 2)
            roots(Q_MEM, D, m_rstd, MEM)

            act.wait_ge(consts_in, 48)
            for kb in range(KB):
                if kb % 2 == 0:
                    act.wait_ge(x_loaded[kb // 2], 16)
                if kb >= 1:
                    act.wait_ge(x_summed, kb)
                act.activation(square[:], x_in[:, kb], ACT.Square).then_inc(x_squared, 1)
                act.activation(act_hi[:, kb], x_in[:, kb], ACT.Copy, scale=const("g_mix", kb)).then_inc(x_rounded, 1)
            roots(Q_X, D, rstd)
            for t in range(2):
                act.wait_ge(memT_done, t + 1)
                act.activation(mem_v[:, t], bank[4 + t], ACT.Copy).then_inc(memv_ready, 1)

            def swap_halves(n):
                act.wait_ge(g_evac, NCH * (Z_RQ + n + 1))
                if n:
                    act.wait_ge(swap_used, n)
                for r in range(0, P, 64):
                    act.activation(swap[r:r + 32], z[r + 32:r + 64, Z_RQ + n], ACT.Copy).then_inc(swapped, 1)
                    act.activation(swap[r + 32:r + 64], z[r:r + 32, Z_RQ + n], ACT.Copy).then_inc(swapped, 1)

            for n in range(2):
                act.wait_ge(g_evac, NCH * (Z_CQ + n + 1))
                act.wait_ge(lora_summed, n) if n else act.wait_ge(x_summed, KB)
                act.activation(square[:], z[:, Z_CQ + n], ACT.Square).then_inc(lora_squared, 1)
            act.wait_ge(lora_summed, 2)
            swap_halves(0)
            roots(Q_CQ, QL, sumsq)
            swap_halves(1)
            act.wait_ge(lora_normed, 2)
            act.activation(sumsq[:], z[:, Z_CKV], ACT.Square).then_inc(lora_squared, 1)
            swap_halves(2)
            swap_halves(3)
            roots(Q_CKV, KVL, sumsq)
            act.wait_ge(g_evac, NCH * (Z_RG + 2))
            act.activation(z[:, Z_RG:Z_RG + 2], z[:, Z_RG:Z_RG + 2], ACT.Silu).then_inc(gated, 1)
            act.wait_ge(w_used, W_OUT)
            for c in range(NT):
                act.wait_ge(tokT_done, 3 * c + 2)
                act.activation(rv_tok[:, c], bank[2 + c % 2].rearrange("p (h d) -> p h d", h=4)[:, :, HD:P],
                               ACT.Copy).then_inc(tok_ready, 1)
                act.wait_ge(tokT_done, 3 * c + 3)
                act.activation(sv_tok[:, c], bank[4 + c % 2].rearrange("p (h d) -> p h d", h=4)[:, :, HD:P],
                               ACT.Copy).then_inc(tok_ready, 1)
            for c in range(NT):
                act.wait_ge(ret_o, c + 1)
                act.wait_ge(ret_q, c + 1)
                act.activation(z[:, Z_RQ:Z_RQ + 2, tile(c)], bank[4 + c % 2][:, 0:2 * P].rearrange(
                    "p (a n) -> p a n", a=2), ACT.Copy).then_inc(ret_o_evac, 1)
            for p in range(2):
                act.wait_ge(sum_used, Q_HEAD + 6 * p + 3)
                if p:
                    act.wait_ge(sum_ready, Q_HEAD + 6)
                    act.wait_ge(ret_done, 2)
                else:
                    act.wait_ge(stored_state, 16)
                act.activation(square[:], z[:, Z_RQ + p], ACT.Square).then_inc(head_squared, 1)
                roots(Q_HEAD + 6 * p + 3, 1, sumsq)
            act.wait_ge(kpe_rotated, 1)
            act.activation(rope_tmp[:, 0], z[96:P, Z_KPE], ACT.Copy).then_inc(kpe_swapped, 1)
            act.wait_ge(kpe_ready, 1)
            for hh in range(2):
                act.activation(k_pass[64:96, hh], z[64:96, Z_KPE, 0:TP], ACT.Copy)

            def mla_exp(n, slot, m, width):
                act.wait_ge(row_max, m + 1)
                act.activation(prob[:, n % 3, 0:width], S[slot][:, 0:width], ACT.Exp, bias=neg_max[:, n % 4:n % 4 + 1],
                               accum_out=row_sum[:, n % 4:n % 4 + 1]).then_inc(exp_done, 1)

            def sb_softplus(slot, t, width):
                act.wait_ge(s_ready, t + 1)
                own_a(act.activation(log_term[:, 0:width], S[slot][:, 0:width], ACT.Abs))
                own_a.settle()
                own_a(act.activation(log_term[:, 0:width], log_term[:, 0:width], ACT.Exp, scale=-1.0))
                own_a.settle()
                act.activation(log_term[:, 0:width], log_term[:, 0:width], ACT.Ln, bias=1.0).then_inc(sb_log, 1)

            def sb_exp(slot, u, width):
                act.wait_ge(sb_arg, u + 1)
                act.activation(prob[:, slot, 0:width], soft[:, 0:width], ACT.Exp).then_inc(sb_p, 1)

            def copy_transposed(g, ring, blocks, reused):
                act.wait_ge(pt_done, g + 1)
                if reused:
                    act.wait_ge(pv_done, g - 2)
                act.activation(probT[:, ring % 3, 0:blocks * P], bank[4 + ring % 2][:, 0:blocks * P],
                               ACT.Copy).then_inc(pt_copied, 1)

            with act.Fori(0, NP) as i:
                own_a.enter(i, 2 * NTILE)
                for c in range(2):
                    act.wait_ge(pass_done, 12 * i + 4 * c + 4)
                    act.activation(k_pass[0:64, 0, 512 * c:512 * c + 512], bank[3][0:64], ACT.Copy)
                    act.activation(k_pass[0:64, 1, 512 * c:512 * c + 512], bank[3][64:P], ACT.Copy).then_inc(kv_evac, 1)
                    if c == 0:
                        act.activation(sb_q[0:HD], z[0:HD, bass.ds(Z_SQ + i, 1), 0:TP].rearrange("p a n -> p (a n)"),
                                       ACT.Copy, scale=HD ** -0.5).then_inc(sb_staged, 1)
                        act.activation(sv_pass[:], sv_tok[:, 0:NTILE, bass.ds(i, 1)].rearrange("p c a d -> p c (a d)"),
                                       ACT.Copy).then_inc(sb_staged, 1)
                    act.wait_ge(q_evac, 6 * i + 3 * c + 3)
                    act.activation(rope_tmp[:, c], q_pass[96:P, c], ACT.Copy).then_inc(q_swapped, 1)
                for c in range(2):
                    act.wait_ge(pass_done, 12 * i + 9 + c)
                    act.activation(v_pass[:, 4 * c:4 * c + 4], bank[c].rearrange("p (c n) -> p c n", c=4),
                                   ACT.Copy).then_inc(kv_evac, 1)
                for hh in range(2):
                    act.wait_ge(pass_done, 12 * i + 11 + hh)
                    act.wait_ge(kpe_ready, 1)
                    act.activation(q_abs[:, :, bass.ds(2 * i + hh, 1)].rearrange("p b a t -> p b (a t)"),
                                   bank[2 + hh][:, 0:TS].rearrange("p (b t) -> p b t", b=DB), ACT.Copy).then_inc(kv_evac, 1)
                    act.wait_ge(q_ready, 2 * i + 2)
                    act.wait_ge(stored_skv, 16)
                    act.activation(q_pe[:, :, bass.ds(2 * i + hh, 1)].rearrange("p b a t -> p b (a t)"),
                                   q_pass[64:96, hh, TP:T].rearrange("p (b t) -> p b t", b=DB), ACT.Copy)
                for n in range(N_LOOP + 2):
                    if n < N_LOOP:
                        kind, j = KINDS[n]
                        if kind < 2:
                            if n >= 3:
                                act.wait_ge(pt_done, G_PASS * i + G_BEFORE[n - 2])
                            mla_exp(n, n % 2, 16 * i + 2 * j + kind, P * j + P)
                        else:
                            sb_softplus(n % 2, N_LOOP * i + n, P * j + P)
                    if 1 <= n <= N_LOOP and KINDS[n - 1][0] == 2:
                        j = KINDS[n - 1][1]
                        if n - 1 >= 3:
                            act.wait_ge(pt_done, G_PASS * i + G_BEFORE[n - 3])
                        sb_exp(2, 8 * i + j, P * j + P)
                    if n >= 2:
                        kind, j = KINDS[n - 2]
                        for g in range(G_BEFORE[n - 2], G_BEFORE[n - 1]):
                            copy_transposed(G_PASS * i + g, g, min(4, j + 1 - 4 * (g - G_BEFORE[n - 2])), g >= 3)
                        act.wait_ge(pv_done, G_PASS * i + G_BEFORE[n - 1])
                        act.wait_ge(kpe_ready, 1)
                        rows = slice(64, P) if kind == 1 else slice(0, 64)
                        act.activation(mixed[rows, bass.ds(i + (4 if kind == 2 else 0), 1), tile(j)].rearrange(
                            "p a n -> p (a n)"), bank[6 + n % 2][rows, 0:P], ACT.Copy).then_inc(o_evac, 1)
                own_a.leave(NP)
            def copy_output(t, dst, src):
                act.activation(dst, src, ACT.Copy).then_inc(o_evac, 1)

            act.wait_ge(new_done, 1)
            act.activation(ckv_new[:], bank[4][:, 0:P], ACT.Copy).then_inc(new_ready, 1)
            width = PAST + TS
            for n in range(DB + 1):
                if n < DB:
                    if n >= 3:
                        act.wait_ge(pt_done, G_MLA_S + 2 * (n - 2))
                    mla_exp(n, n % 2, 2 * NP * NTILE + n, width)
                if n >= 1:
                    b = n - 1
                    for g in range(2):
                        copy_transposed(G_MLA_S + 2 * b + g, 2 * b + g, (4, 1)[g], True)
                    act.wait_ge(pv_done, G_MLA_S + 2 * b + 2)
                    copy_output(b, o_lat[:, b], bank[6 + b % 2][:, 0:P].rearrange("p (h t) -> p h t", h=MH))
            act.wait_ge(setup_done, 5)
            for h in range(SH):
                last = act.activation(sk_new[64 * (h % 2):64 * (h % 2) + 64, h // 2], z[0:HD, Z_SK + h, TP:T], ACT.Copy)
            last.then_inc(sk_new_ready, 1)

            def pair_queries(p):
                if p >= 2:
                    act.wait_ge(s_ready, T_SB_S + p - 1)
                for bb in range(2):
                    for h in range(SH):
                        rows = slice(64 * (h % 2), 64 * (h % 2) + 64)
                        at = 64 * bb + DS * h
                        frame = TP + DS * (2 * p + bb)
                        last = act.activation(sb_pair[rows, p % 2, bb, h // 2, at:at + DS],
                                              z[0:HD, Z_SQ + h, frame:frame + DS], ACT.Copy, scale=HD ** -0.5)
                last.then_inc(sb_pair_ready, 1)

            pair_queries(0)
            pair_queries(1)
            act.wait_ge(o_heads, 1)
            act.activation(mixed[:, 0:4, TP:T], bank[7].rearrange("p (h n) -> p h n", h=4), ACT.Copy).then_inc(o_sample, 1)
            for n in range(DB // 2 + 1):
                if n < DB // 2:
                    act.wait_ge(sb_arg, NP * NTILE + n)
                    sb_softplus(n % 2, T_SB_S + n, width)
                if n >= 1:
                    p = n - 1
                    act.wait_ge(pt_done, G_SB_S + 2 * max(0, p - 2))
                    sb_exp(p % 3, NP * NTILE + p, width)
                    if n + 1 < DB // 2:
                        pair_queries(n + 1)
                    for g in range(2):
                        copy_transposed(G_SB_S + 2 * p + g, 1 + 2 * p + g, (4, 1)[g], True)
                    act.wait_ge(pv_done, G_SB_S + 2 * p + 2)
                    out = bank[6 + p % 2][:, 0:256].rearrange("p (b f n) -> p b f n", b=2, f=2)
                    for h in range(SH):
                        rows = slice(64 * (h % 2), 64 * (h % 2) + 64)
                        last = act.activation(mixed[0:64, 4 + h, TP + 2 * DS * p:TP + 2 * DS * (p + 1)].rearrange(
                            "p (b t) -> p b t", b=2), out[rows, :, h // 2, DS * h:DS * h + DS], ACT.Copy)
                    last.then_inc(o_evac, 1)

            act.wait_ge(pv_done, G_SAMPLE_END)
            act.wait_ge(o_evac, T_SB_S + DB // 2)
            act.wait_ge(ret_done, 4)
            for k in range(2):
                act.dma_start(x_blk[:, k], io["xT"][:, k]).then_inc(xb_in[k], 16)
            for kb in range(KB):
                act.activation(mix_hi[:, kb], mixed[:, kb], ACT.Copy).then_inc(mix_rounded, 1)

            def residual(m, first, src, gain_name):
                act.wait_ge(g_evac, first + NCH * (m + 1))
                if m:
                    act.wait_ge(x_summed, sums_before + m)
                act.activation(square[:], src, ACT.Square).then_inc(x_squared, 1)
                act.activation(act_hi[:, m], src, ACT.Copy, scale=const(gain_name, m)).then_inc(x_rounded, 1)

            sums_before = KB
            act.wait_ge(mix_split, KB)
            for m in range(KB):
                residual(m, G_OUT, x_blk[:, m % 2], "g_mem_q")
                act.dma_start(io["x_mid"][:, m], x_blk[:, m % 2]).then_inc(xb_out[m % 2], 16)
                if m >= 1 and m + 1 < KB:
                    act.wait_ge(xb_out[(m - 1) % 2], 16 * ((m - 1) // 2 + 1))
                    act.wait_ge(x_split, sums_before + m)
                    act.dma_start(x_blk[:, (m + 1) % 2], io["xT"][:, m + 1]).then_inc(xb_in[(m + 1) % 2], 16)
            roots(Q_MQ, D, rstd)

            def memory_exp(n, heads):
                act.wait_ge(m_row_max, n + 1)
                if n >= 2:
                    act.wait_ge(mt_done, 2 * (n - 1))
                for h in range(heads):
                    last = act.activation(m_prob[:, n % 2, h * MEM:h * MEM + MEM], S[n % 2][:, h * MEM:h * MEM + MEM],
                                          ACT.Exp, bias=m_max[:, n % 2, h:h + 1], accum_out=m_sum[:, n % 2, h:h + 1])
                last.then_inc(m_exp, 1)

            for n in range(NTILE + DB // 2 + 1):
                if n < NTILE + DB // 2:
                    memory_exp(n, GH if n < NTILE else 1)
                    p = n - NTILE + 2
                    if 0 <= p < DB // 2:
                        act.wait_ge(qm_zero, 1)
                        act.wait_ge(g_evac, G_MO)
                        if p >= 2:
                            act.wait_ge(ms_ready, n + 1)
                        for bb in range(2):
                            for h in range(GH):
                                at, frame = 64 * bb + DS * h, TP + DS * (2 * p + bb)
                                last = act.activation(qm_pair[:, p % 2, bb, h, at:at + DS],
                                                      qm[:, h, frame:frame + DS], ACT.Copy)
                        last.then_inc(qm_pair_ready, 1)
                if n >= 1:
                    c = n - 1
                    for g in range(2):
                        act.wait_ge(mt_done, 2 * c + g + 1)
                        if c >= 2:
                            act.wait_ge(m_pv, c - 1)
                        w = 512 if c < NTILE else P
                        act.activation(m_probT[:, 2 * (c % 2) + g, 0:w], bank[4 + g][:, 0:w], ACT.Copy).then_inc(mt_copied, 1)
                    act.wait_ge(m_pv, c + 1)
                    at, w = (P * c, P) if c < NTILE else (TP + 2 * DS * (c - NTILE), 2 * DS)
                    act.activation(om_hi[:, :, at:at + w], bank[6 + c % 2][:, 0:GH * w].rearrange(
                        "p (h n) -> p h n", h=GH), ACT.Copy).then_inc(om_rounded, 1)

            sums_before = 2 * KB
            for m in range(KB):
                residual(m, G_MO, x[:, m], "g_ffn")
            roots(Q_FFN, D, rstd)

            def first_tap(m, ab):
                act.wait_ge(g_evac, G_UP + NCH * (2 * m + ab + 1))
                act.wait_ge(conv0_in, 16)
                blk = m + NFF * ab
                saved = conv_new[:, bass.ds(blk, 1)].rearrange("p a n -> p (a n)")
                act.activation(saved[:, 0:2], ext[:, ab, TP:TP + 2], ACT.Copy)
                act.activation(saved[:, 2:].rearrange("p (b r) -> p b r", b=DB), sample_rows(ext[:, ab], DS, 2), ACT.Copy)
                act.activation(conv[:, ab, 0:EXT - 2], ext[:, ab, 0:EXT - 2], ACT.Identity, bias=conv_bias(blk),
                               scale=conv_tap(blk, 0)).then_inc(tap0_done, 1)

            def activate(m):
                act.wait_ge(conv_done, 2 * m + 1)
                act.wait_ge(conv0_in, 16)
                act.activation(conv[:, 0, 0:EXT - 2], conv[:, 0, 0:EXT - 2], ACT.Silu).then_inc(silu_done, 1)

            def round_product(m, kb):
                act.wait_ge(s_product, m + 1)
                act.wait_ge(conv0_in, 16)
                act.activation(s_hi[:, kb, 0:TP], conv[:, 0, 0:TP], ACT.Copy)
                act.activation(s_hi[:, kb, TP:T].rearrange("p (b t) -> p b t", b=DB), sample_rows(conv[:, 0], 0, DS),
                               ACT.Copy).then_inc(s_rounded, 1)

            with act.Fori(0, NGRP) as i:
                for kb in range(2):
                    first_tap(2 * i + kb, 0)
                    activate(2 * i + kb)
                    first_tap(2 * i + kb, 1)
                    round_product(2 * i + kb, kb)
            for m in range(KB):
                act.wait_ge(d_evac, 3 * KB * (NGRP - 1) + 3 * (m + 1))
                if m:
                    act.wait_ge(x_summed, 3 * KB + m)
                act.activation(square[:], x[:, m], ACT.Square).then_inc(x_squared, 1)
            roots(Q_FINAL, D, rstd)

        @block.vector
        def _(dve):
            own_v = Own(dve, dve_own)

            dve.memset(ones[:], 1.0).then_inc(setup_done, 1)
            dve.memset(eps[:], EPS).then_inc(setup_done, 1)
            dve.wait_ge(m_loaded, 16)
            dve.wait_ge(consts_in, 48)
            dve.wait_ge(m_squared, 1)
            for kb in range(KB):
                last = dve.tensor_scalar(m_in[:, kb], m_in[:, kb], const("g_mem_kv", kb), None, ALU.mult)
            last.then_inc(m_gained, 1)
            dve.wait_ge(m_rounded, 1)
            dve.wait_ge(m_gained, 1)
            dve.tensor_tensor(m_lo[:], m_in[:], m_hi[:].bitcast(F32), ALU.subtract).then_inc(m_split, 1)
            dve.wait_ge(sum_used, Q_MEM + 1)
            dve.reciprocal(m_rstd[:], m_rstd[:]).then_inc(rstd_ready, 1)

            for kb in range(KB):
                dve.wait_ge(x_squared, kb + 1)
                if kb:
                    dve.wait_ge(x_summed, kb)
                    dve.tensor_tensor(sumsq[:], sumsq[:], square[:], ALU.add).then_inc(x_summed, 1)
                else:
                    dve.tensor_copy(sumsq[:], square[:]).then_inc(x_summed, 1)
                dve.wait_ge(x_rounded, kb + 1)
                dve.scalar_tensor_tensor(act_lo[:, kb], x_in[:, kb], const("g_mix", kb), act_hi[:, kb].bitcast(F32),
                                         ALU.mult, ALU.subtract).then_inc(x_split, 1)

            dve.wait_ge(rstd_ready, 1)
            with dve.Fori(0, 4) as i:
                for k in range(2):
                    dve.wait_ge(w_used, W_MEM + 2 * i + k + 1)
                    dve.tensor_tensor(mkv[:, bass.ds(2 * i + k, 1)].rearrange("p a n -> p (a n)"),
                                      bank[4 + k][:, 0:MEM], m_rstd[:], ALU.mult).then_inc(mem_evac, 1)
            dve.wait_ge(sum_used, Q_X + 3)
            dve.reciprocal(rstd[:], rstd[:]).then_inc(rstd_ready, 1)
            dve.wait_ge(rstd_ready, 2)

            def z_evacuate(b, k):
                for c in range(NCH):
                    chunk_done(dve, W_IN + b, 2 * b, c)
                    dst = z[:, bass.ds(b, 1), frames(c)].rearrange("p a n -> p (a n)")
                    dve.tensor_tensor(dst, bank[3 * k + c][:, 0:CH], rstd[:, frames(c)], ALU.mult).then_inc(g_evac, 1)

            def rotate(n):
                scale = 1.0 if n < 2 else HD ** -0.5
                dve.wait_ge(swapped, 4 * n + 4)
                dve.wait_ge(g_evac, NCH * (Z_RQ + n + 1))
                blk = z[:, Z_RQ + n]
                own_v(dve.scalar_tensor_tensor(blk, blk, scale, rope_cos[:], ALU.mult, ALU.mult))
                own_v(dve.scalar_tensor_tensor(swap[:], swap[:], scale, rope_sin[:], ALU.mult, ALU.mult))
                own_v.settle()
                dve.tensor_tensor(blk, blk, swap[:], ALU.add).then_inc(swap_used, 1)

            def norm_latent(first, n_blocks, q, gain_name):
                dve.wait_ge(sum_used, q + 3)
                own_v(dve.reciprocal(sumsq[:], sumsq[:]))
                own_v.settle()
                for n in range(n_blocks):
                    dve.scalar_tensor_tensor(z[:, first + n], z[:, first + n], const(gain_name, n), sumsq[:],
                                             ALU.mult, ALU.mult).then_inc(lora_normed, 1)

            with dve.Fori(0, 2) as i:
                for k in range(2):
                    z_evacuate(2 * i + k, k)
            z_evacuate(4, 0)
            dve.wait_ge(lora_squared, 1)
            dve.tensor_copy(sumsq[:], square[:]).then_inc(lora_summed, 1)
            z_evacuate(5, 1)
            dve.wait_ge(lora_squared, 2)
            dve.wait_ge(lora_summed, 1)
            dve.tensor_tensor(sumsq[:], sumsq[:], square[:], ALU.add).then_inc(lora_summed, 1)
            for b in range(6, 10):
                z_evacuate(b, b % 2)
            dve.wait_ge(rope_in, 32)
            rotate(0)
            z_evacuate(10, 0)
            norm_latent(Z_CQ, 2, Q_CQ, "g_q")
            z_evacuate(11, 1)
            rotate(1)
            z_evacuate(12, 0)
            rotate(2)
            z_evacuate(13, 1)
            rotate(3)
            z_evacuate(14, 0)
            z_evacuate(15, 1)
            dve.wait_ge(swap_used, 4)
            z_evacuate(16, 0)
            norm_latent(Z_CKV, 1, Q_CKV, "g_kv")
            z_evacuate(17, 1)

            dve.wait_ge(ret_in, 80)
            for c in range(NT):
                dve.wait_ge(tokT_done, 3 * c + 1)
                dve.tensor_tensor(kd_tok[:, c], bank[c % 2][:, 0:RH * HD].rearrange("p (h d) -> p h d", h=RH),
                                  k_decay[:, c // NTILE], ALU.mult).then_inc(kd_ready, 1)
            dve.wait_ge(swap_used, 4)
            dve.wait_ge(lora_normed, 3)
            dve.memset(state[:], 0.0).then_inc(setup_done, 1)
            dve.wait_ge(tok_ready, 2 * NT)
            for p in range(2):
                v = rv_tok[:, NTILE, 2 * p:2 * p + 2].rearrange("p h d -> p (h d)")
                for b in range(DB):
                    ins = dve.tensor_scalar(v_own[:, p, b], v, own[:, b:b + 1], None, ALU.mult)
                ins.then_inc(v_own_ready, 1)
            dve.wait_ge(setup_done, 3)
            for c in range(NT):
                dve.wait_ge(ret_scores, c + 1)
                if c >= 2:
                    dve.wait_ge(ret_o, c - 1)
                dve.tensor_tensor(kept[:, c % 2], S[c % 2][:].rearrange("p (h n) -> p h n", h=2)[:, :, 0:2 * P],
                                  ret_mask[:, c // NTILE], ALU.mult).then_inc(ret_kept, 1)
                dve.tensor_tensor(q_dec[:, c % 2], z[:, Z_RQ:Z_RQ + 2, tile(c)], q_decay[:, c // NTILE],
                                  ALU.mult).then_inc(ret_q, 1)
                if c < NTILE:
                    dve.wait_ge(ret_kv, c + 1)
                    dve.wait_ge(ret_o, c + 1)
                    if c:
                        dve.wait_ge(ret_state, c)
                    for p in range(2):
                        for b, rows in halves(p):
                            ins = dve.scalar_tensor_tensor(
                                state[rows, p, rows], state[rows, p, rows], const("decay128", p, rows=rows),
                                bank[6 + c % 2][rows, p * P + rows.start:p * P + rows.start + HD], ALU.mult, ALU.add)
                    ins.then_inc(ret_state, 1)
            dve.wait_ge(ret_o, NT)
            for p in range(2):
                for half in range(2):
                    dve.wait_ge(ret_kv, NTILE + 2 * p + half + 1)
                    for _, rows in halves(p):
                        at = rows.start
                        src = bank[2 * p + half].rearrange("p (b n) -> p b n", b=4)[rows, :, at:at + HD]
                        dst = s0[rows, 4 * half:4 * half + 4, p, at:at + HD]
                        dve.scalar_tensor_tensor(dst, dst, const("decay16", p, rows=rows), src, ALU.mult,
                                                 ALU.add).then_inc(s0_new, 1)
            for p in range(2):
                for n, b, at, w in sum_chunks(Q_HEAD + 6 * p):
                    dve.wait_ge(sum_ready, n + 1)
                    dve.wait_ge(ret_o_evac, NT)
                    dve.tensor_tensor(z[:, Z_RQ + p, at:at + w], z[:, Z_RQ + p, at:at + w], bank[b][:, 0:w],
                                      ALU.subtract).then_inc(sum_used, 1)
                dve.wait_ge(sum_used, Q_HEAD + 6 * p + 6)
                own_v(dve.reciprocal(sumsq[:], sumsq[:]))
                own_v.settle()
                own_v(dve.scalar_tensor_tensor(z[:, Z_RQ + p], z[:, Z_RQ + p], const("g_ret", p), sumsq[:],
                                               ALU.mult, ALU.mult))
                own_v.settle()
                dve.wait_ge(gated, 1)
                for hh, (_, rows) in enumerate(halves(p)):
                    dve.tensor_tensor(mixed[HD:P, 4 + 2 * p + hh], z[rows, Z_RQ + p], z[rows, Z_RG + p],
                                      ALU.mult).then_inc(ret_done, 1)
            dve.wait_ge(attn_in, 32)
            dve.wait_ge(ret_done, 4)
            dve.memset(sb_q[HD:P], 0.0).then_inc(setup_done, 1)
            dve.tensor_tensor(z[64:P, Z_KPE], z[64:P, Z_KPE], rope_pe[64:P], ALU.mult).then_inc(kpe_rotated, 1)
            dve.wait_ge(kpe_swapped, 1)
            dve.wait_ge(kpe_rotated, 1)
            dve.tensor_tensor(z[64:96, Z_KPE], z[64:96, Z_KPE], rope_tmp[:, 0], ALU.add).then_inc(kpe_ready, 1)

            def mla_max(n, slot, t, width, masked):
                dve.wait_ge(s_ready, t + 1)
                own_v(masked())
                own_v.settle()
                dve.tensor_reduce(neg_max[:, n % 4:n % 4 + 1], S[slot][:, 0:width], AX.X, ALU.max,
                                  negate=True).then_inc(row_max, 1)

            def mla_norm(n, m, width):
                dve.wait_ge(exp_done, m + 1)
                own_v(dve.reciprocal(row_sum[:, n % 4:n % 4 + 1], row_sum[:, n % 4:n % 4 + 1]))
                own_v.settle()
                dve.tensor_scalar(prob[:, n % 3, 0:width], prob[:, n % 3, 0:width], row_sum[:, n % 4:n % 4 + 1], None,
                                  ALU.mult).then_inc(p_norm, 1)

            def sb_exponent(slot, u, width, keep, hide, reused):
                last = slice(width - P, width)
                dve.wait_ge(sb_log, u + 1)
                if reused:
                    dve.wait_ge(sb_p, u)
                sp_ = soft[:, 0:width]
                own_v(dve.scalar_tensor_tensor(sp_, S[slot][:, 0:width], 0.0, log_term[:, 0:width], ALU.max, ALU.add))
                own_v.settle()
                own_v(dve.tensor_tensor(soft[:, last], soft[:, last], keep, ALU.mult))
                own_v.settle()
                one = ones[:, 0:1].to_broadcast([P, width])
                own_v(dve.tensor_tensor_scan(sp_[:, ::-1], one, sp_[:, ::-1], 0.0, ALU.mult, ALU.add))
                own_v.settle()
                own_v(dve.tensor_tensor(sp_, S[slot][:, 0:width], sp_, ALU.subtract))
                own_v.settle()
                dve.tensor_tensor(soft[:, last], soft[:, last], hide, ALU.add).then_inc(sb_arg, 1)

            with dve.Fori(0, NP) as i:
                own_v.enter(i, 2 * 16 + 4 * 8)
                for hh in range(2):
                    for c in range(NCH):
                        dve.wait_ge(pass_done, 12 * i + 4 * hh + c + 1)
                        dve.scalar_tensor_tensor(q_pass[:, hh, frames(c)], bank[c][:, 0:CH], MLA_SCALE,
                                                 rope_pe[:, frames(c)], ALU.mult, ALU.mult).then_inc(q_evac, 1)
                    dve.wait_ge(q_swapped, 2 * i + hh + 1)
                    dve.tensor_tensor(q_pass[64:96, hh], q_pass[64:96, hh], rope_tmp[:, hh], ALU.add).then_inc(q_ready, 1)
                for n in range(N_LOOP + 1):
                    if n < N_LOOP:
                        kind, j = KINDS[n]
                        width = P * j + P
                        if kind < 2:
                            mla_max(n, n % 2, N_LOOP * i + n, width,
                                    lambda: dve.memset(S[n % 2][0:64, width - 64:width], NEG))
                    if n >= 1:
                        kind, j = KINDS[n - 1]
                        if kind < 2:
                            mla_norm(n - 1, 16 * i + 2 * j + kind, P * j + P)
                        else:
                            sb_exponent((n - 1) % 2, 8 * i + j, P * j + P, before[:, 0], before[:, 1], j > 0)
                own_v.leave(NP)
            dve.wait_ge(sample_in, 64)
            width = PAST + TS
            new = slice(PAST, width)
            for n in range(DB + 1):
                if n < DB:
                    band = own_band[:, DS * (DB - 1 - n):DS * (DB - 1 - n) + TS]
                    mla_max(n, n % 2, T_MLA_S + n, width,
                            lambda: dve.tensor_tensor(S[n % 2][:, new], S[n % 2][:, new], band, ALU.add))
                if n >= 1:
                    mla_norm(n - 1, 2 * NP * NTILE + n - 1, width)
            dve.memset(sb_pair[:], 0.0).then_inc(setup_done, 1)
            for p in range(DB // 2):
                at = DS * (DB - 2 - 2 * p)
                sb_exponent(p % 2, NP * NTILE + p, width, keep_band[:, at:at + TS], hide_band[:, at:at + TS], True)

            for kb in range(KB):
                dve.wait_ge(mix_rounded, kb + 1)
                dve.tensor_tensor(mix_lo[:, kb], mixed[:, kb], mix_hi[:, kb].bitcast(F32),
                                  ALU.subtract).then_inc(mix_split, 1)

            def residual(m, count, src, gain_name):
                dve.wait_ge(x_squared, count + m + 1)
                if m:
                    dve.wait_ge(x_summed, count + m)
                    dve.tensor_tensor(sumsq[:], sumsq[:], square[:], ALU.add).then_inc(x_summed, 1)
                else:
                    dve.tensor_copy(sumsq[:], square[:]).then_inc(x_summed, 1)
                dve.wait_ge(x_rounded, count + m + 1)
                dve.scalar_tensor_tensor(act_lo[:, m], src, const(gain_name, m), act_hi[:, m].bitcast(F32),
                                         ALU.mult, ALU.subtract).then_inc(x_split, 1)

            for m in range(KB):
                dve.wait_ge(xb_in[m % 2], 16 * (m // 2 + 1))
                for c in range(NCH):
                    chunk_done(dve, W_OUT + m, 2 * NZ + 2 * m, c)
                    dve.tensor_tensor(x_blk[:, m % 2, frames(c)], bank[3 * (m % 2) + c][:, 0:CH],
                                      x_blk[:, m % 2, frames(c)], ALU.add).then_inc(g_evac, 1)
                residual(m, KB, x_blk[:, m % 2], "g_mem_q")
            dve.wait_ge(sum_used, Q_MQ + 3)
            dve.reciprocal(rstd[:], rstd[:]).then_inc(rstd_ready, 1)
            dve.wait_ge(rstd_ready, 3)
            for m in range(GH):
                for c in range(NCH):
                    chunk_done(dve, W_MQ + m, 2 * (NZ + KB + m), c)
                    dve.scalar_tensor_tensor(qm[:, m, frames(c)], bank[3 * (m % 2) + c][:, 0:CH], MEM_SCALE,
                                             rstd[:, frames(c)], ALU.mult, ALU.mult).then_inc(g_evac, 1)
            dve.wait_ge(w_used, W_MO)
            dve.memset(qm_pair[:], 0.0).then_inc(qm_zero, 1)

            for n in range(NTILE + DB // 2 + 2):
                heads = GH if n < NTILE else 1
                if n < NTILE + DB // 2:
                    dve.wait_ge(ms_ready, n + 1)
                    dve.tensor_reduce(m_max[:, n % 2, 0:heads], S[n % 2][:, 0:heads * MEM].rearrange(
                        "p (h k) -> p h k", h=heads), AX.X, ALU.max, negate=True).then_inc(m_row_max, 1)
                if 1 <= n <= NTILE + DB // 2:
                    c = n - 1
                    heads = GH if c < NTILE else 1
                    dve.wait_ge(m_exp, c + 1)
                    own_v(dve.reciprocal(m_sum[:, c % 2, 0:heads], m_sum[:, c % 2, 0:heads]))
                    own_v.settle()
                    pr = m_prob[:, c % 2, 0:heads * MEM].rearrange("p (h k) -> p h k", h=heads)
                    dve.tensor_tensor(pr, pr, m_sum[:, c % 2, 0:heads].unsqueeze(2).to_broadcast([P, heads, MEM]),
                                      ALU.mult).then_inc(m_norm, 1)
                if n >= 2:
                    c = n - 2
                    at, w = (P * c, P) if c < NTILE else (TP + 2 * DS * (c - NTILE), 2 * DS)
                    dve.wait_ge(om_rounded, c + 1)
                    dve.tensor_tensor(om_lo[:, :, at:at + w], bank[6 + c % 2][:, 0:GH * w].rearrange(
                        "p (h n) -> p h n", h=GH), om_hi[:, :, at:at + w].bitcast(F32), ALU.subtract).then_inc(om_split, 1)

            dve.wait_ge(x_in_again, 16)
            for m in range(KB):
                for c in range(NCH):
                    n = 6 * (m // 2) + 3 * (m % 2) + c
                    if n % 6 < 5:
                        dve.wait_ge(g_done, 2 * (NZ + KB + GH) + n - n // 6 + 1)
                    else:
                        dve.wait_ge(w_used, W_MO + m // 2 + 1)
                    dve.tensor_tensor(x[:, m, frames(c)], bank[3 * (m % 2) + c][:, 0:CH], x[:, m, frames(c)],
                                      ALU.add).then_inc(g_evac, 1)
                residual(m, 2 * KB, x[:, m], "g_ffn")
            dve.wait_ge(sum_used, Q_FFN + 3)
            dve.reciprocal(rstd[:], rstd[:]).then_inc(rstd_ready, 1)
            dve.wait_ge(rstd_ready, 4)
            dve.memset(ext[:, :, 0:2], 0.0).then_inc(ext_zero, 1)
            dve.wait_ge(ext_zero, 1)
            dve.wait_ge(conv0_in, 16)

            def up_evacuate(m, ab, slot):
                blk = m + NFF * ab
                for c in range(2):
                    chunk_done(dve, slot, UP_BEFORE + 2 * (2 * m + ab), c)
                    dve.tensor_tensor(ext[:, ab, 2 + CH * c:2 + CH * c + CH], bank[3 * ab + c][:, 0:CH],
                                      rstd[:, frames(c)], ALU.mult).then_inc(g_evac, 1)
                chunk_done(dve, slot, UP_BEFORE + 2 * (2 * m + ab), 2)
                n = TP - 2 * CH
                dve.tensor_tensor(ext[:, ab, 2 + 2 * CH:2 + TP], bank[3 * ab + 2][:, 0:n], rstd[:, 2 * CH:TP], ALU.mult)
                dve.tensor_copy(sample_rows(ext[:, ab], 0, 2),
                                conv0[:, bass.ds(blk, 1)].rearrange("p a (b r) -> p (a b) r", b=DB))
                dve.tensor_tensor(sample_rows(ext[:, ab], 2, DS), bank[3 * ab + 2][:, n:CH].rearrange(
                    "p (b t) -> p b t", b=DB), rstd[:, TP:T].rearrange("p (b t) -> p b t", b=DB),
                    ALU.mult).then_inc(g_evac, 1)

            def more_taps(m, ab):
                dve.wait_ge(tap0_done, 2 * m + ab + 1)
                c = conv[:, ab, 0:EXT - 2]
                own_v(dve.scalar_tensor_tensor(c, ext[:, ab, 1:EXT - 1], conv_tap(m + NFF * ab, 1), c, ALU.mult, ALU.add))
                own_v.settle()
                dve.scalar_tensor_tensor(c, ext[:, ab, 2:EXT], conv_tap(m + NFF * ab, 2), c, ALU.mult,
                                         ALU.add).then_inc(conv_done, 1)

            def gate(m, kb):
                dve.wait_ge(silu_done, m + 1)
                dve.wait_ge(conv_done, 2 * m + 2)
                dve.tensor_tensor(conv[:, 0, 0:EXT - 2], conv[:, 0, 0:EXT - 2], conv[:, 1, 0:EXT - 2],
                                  ALU.mult).then_inc(s_product, 1)
                dve.wait_ge(s_rounded, m + 1)
                dve.tensor_tensor(s_lo[:, kb, 0:TP], conv[:, 0, 0:TP], s_hi[:, kb, 0:TP].bitcast(F32), ALU.subtract)
                dve.tensor_tensor(s_lo[:, kb, TP:T].rearrange("p (b t) -> p b t", b=DB), sample_rows(conv[:, 0], 0, DS),
                                  s_hi[:, kb, TP:T].bitcast(F32).rearrange("p (b t) -> p b t", b=DB),
                                  ALU.subtract).then_inc(s_split, 1)

            def down_accumulate(g, slot, after_block=None):
                for m in range(KB):
                    for c in range(NCH):
                        q = NCH * m + c
                        if q % 12 < 11:
                            dve.wait_ge(d_done, 22 * g + q - q // 12 + 1)
                        else:
                            dve.wait_ge(w_used, slot + q // 12 + 1)
                        dve.tensor_tensor(x[:, m, frames(c)], bank[6 + q % 2][:, 0:CH], x[:, m, frames(c)],
                                          ALU.add).then_inc(d_evac, 1)
                    if after_block:
                        after_block(m)

            for kb in range(2):
                for ab in range(2):
                    up_evacuate(kb, ab, W_FFN + 2 * kb + ab)
                    more_taps(kb, ab)
                gate(kb, kb)
            with dve.Fori(1, NGRP) as i:
                own_v.enter(i - 1, 4)
                slot = 6 * i + (W_FFN - 2)
                up_evacuate(2 * i, 0, slot)
                more_taps(2 * i, 0)
                up_evacuate(2 * i, 1, slot + 1)
                down_accumulate(i - 1, slot + 2)
                more_taps(2 * i, 1)
                gate(2 * i, 0)
                for ab in range(2):
                    up_evacuate(2 * i + 1, ab, slot + 4 + ab)
                    more_taps(2 * i + 1, ab)
                gate(2 * i + 1, 1)
                own_v.leave(NGRP - 1)

            def final_sum(m):
                if m >= 0:
                    dve.wait_ge(x_squared, 3 * KB + m + 1)
                    if m:
                        dve.wait_ge(x_summed, 3 * KB + m)
                        dve.tensor_tensor(sumsq[:], sumsq[:], square[:], ALU.add).then_inc(x_summed, 1)
                    else:
                        dve.tensor_copy(sumsq[:], square[:]).then_inc(x_summed, 1)

            down_accumulate(NGRP - 1, NW - 2, lambda m: final_sum(m - 1))
            final_sum(KB - 1)
            dve.wait_ge(sum_used, Q_FINAL + 3)
            dve.reciprocal(rstd[:], rstd[:]).then_inc(rstd_ready, 1)
            dve.wait_ge(rstd_ready, 5)
            for m in range(KB):
                dve.scalar_tensor_tensor(x[:, m], x[:, m], const("g_final", m), rstd[:], ALU.mult,
                                         ALU.mult).then_inc(y_ready, 1)

        @block.tensor
        def _(pe):
            def split_products(out, k, at, n_kb, hi, lo, first=True, last=True):
                for kb in range(n_kb):
                    for n, (w, x) in enumerate(((w_hi, hi), (w_hi, lo), (w_lo, hi))):
                        mm = pe.matmul(out, w[:, k, at + kb], x(kb), start=first and kb == 0 and n == 0,
                                       stop=last and kb == n_kb - 1 and n == 2)
                return mm

            def sums(q, weights, src):
                for n, b, at, w in sum_chunks(q):
                    if n >= 2:
                        pe.wait_ge(sum_used, n - 1)
                    pe.matmul(bank[b][:, 0:w], weights[:], src[:, at:at + w], start=True,
                              stop=True).then_inc(sum_ready, 1)

            pe.wait_ge(setup_done, 2)
            pe.wait_ge(m_squared, 1)
            for kb in range(KB):
                mm = pe.matmul(bank[6][:, 0:MEM], ones[:], m_sq[:, kb], start=kb == 0, stop=kb == KB - 1)
            mm.then_inc(sum_ready, 1)
            pe.wait_ge(m_split, 1)

            def memory_pair(first):
                for k in range(2):
                    pe.wait_ge(w_split, first + k + 1)
                    split_products(bank[4 + k][:, 0:MEM], k, 0, KB, lambda kb: m_hi[:, kb],
                                   lambda kb: m_lo[:, kb]).then_inc(w_used, 1)

            memory_pair(0)
            with pe.Fori(1, 4) as i:
                pe.wait_ge(mem_evac, 2 * i)
                memory_pair(2 * i)
            pe.wait_ge(mem_evac, 8)
            pe.wait_ge(consts_in, 48)
            for t in range(2):
                for h in range(GH):
                    mm = pe.transpose(bank[4 + t][:, h * P:h * P + P], mkv[:, 4 + h, tile(t)], ident[:])
                mm.then_inc(memT_done, 1)
            pe.wait_ge(x_summed, KB)
            sums(Q_X, ones, sumsq)
            pe.wait_ge(x_split, KB)
            pe.wait_ge(memv_ready, 2)

            def projection(k, slot, evacuated, hi, lo):
                pe.wait_ge(w_split, slot + 1)
                for c in range(NCH):
                    if evacuated is not None:
                        pe.wait_ge(g_evac, evacuated + c + 1)
                    mm = split_products(bank[3 * k + c][:, 0:CH], k, 0, KB, lambda kb: hi[:, kb, frames(c)],
                                        lambda kb: lo[:, kb, frames(c)])
                    mm.then_inc(g_done if c < NCH - 1 else w_used, 1)

            def input_blocks(first, last):
                with pe.Fori(first // 2, last // 2) as i:
                    for k in range(2):
                        projection(k, W_IN + 2 * i + k, 3 * (2 * i + k - 2), act_hi, act_lo)

            for k in range(2):
                projection(k, W_IN + k, None, act_hi, act_lo)
            input_blocks(2, 8)
            pe.wait_ge(lora_summed, 2)
            sums(Q_CQ, ones, sumsq)
            input_blocks(8, 14)
            pe.wait_ge(lora_squared, 3)
            sums(Q_CKV, ones, sumsq)
            input_blocks(14, NZ)
            pe.wait_ge(g_evac, NZ * NCH)
            pe.wait_ge(swap_used, 4)
            for c in range(NT):
                for j, (b, first, n) in enumerate(((c % 2, Z_RK, 2), (2 + c % 2, Z_SK, 4), (4 + c % 2, Z_SQ, 4))):
                    if c >= 2:
                        pe.wait_ge(kd_ready, c - 1) if j == 0 else pe.wait_ge(tok_ready, 2 * (c - 2) + j)
                    for m in range(n):
                        mm = pe.transpose(bank[b][:, m * P:m * P + P], z[:, first + m, tile(c)], ident[:])
                    mm.then_inc(tokT_done, 1)

            def ret_score(c):
                if c >= 2:
                    pe.wait_ge(ret_kept, c - 1)
                for p in range(2):
                    for hh, (_, rows) in enumerate(halves(p)):
                        mm = pe.matmul(S[c % 2][:, 512 * hh + P * p:512 * hh + P * p + P], z[rows, Z_RK + p, tile(c)],
                                       z[rows, Z_RQ + p, tile(c)], start=True, stop=True)
                mm.then_inc(ret_scores, 1)

            pe.wait_ge(kd_ready, NT)
            pe.wait_ge(tok_ready, 2 * NT)
            ret_score(0)
            for c in range(NT):
                if c + 1 < NT:
                    ret_score(c + 1)
                if c < NTILE:
                    if c >= 2:
                        pe.wait_ge(ret_state, c - 1)
                    for p in range(2):
                        mm = pe.matmul(bank[6 + c % 2][:, tile(p)], kd_tok[:, c, 2 * p:2 * p + 2],
                                       rv_tok[:, c, 2 * p:2 * p + 2], start=True, stop=True)
                    mm.then_inc(ret_kv, 1)
                pe.wait_ge(ret_kept, c + 1)
                pe.wait_ge(ret_q, c + 1)
                if c >= 2:
                    pe.wait_ge(ret_o_evac, c - 1)
                if c:
                    pe.wait_ge(ret_state, min(c, NTILE))
                for p in range(2):
                    out = bank[4 + c % 2][:, tile(p)]
                    for hh, (_, rows) in enumerate(halves(p)):
                        mm = pe.matmul(out[rows], rv_tok[:, c, 2 * p + hh], kept[:, c % 2, hh, tile(p)],
                                       start=True, stop=True)
                    if 0 < c < NTILE:
                        mm = pe.matmul(out, state[:, p], q_dec[:, c % 2, p], start=False, stop=True,
                                       skip_group_check=True)
                    if c == NTILE:
                        for b in range(DB):
                            mm = pe.matmul(out[:, b * DS:b * DS + DS], s0[:, b, p],
                                           q_dec[:, c % 2, p, b * DS:b * DS + DS], start=False, stop=True,
                                           skip_group_check=True)
                mm.then_inc(ret_o, 1)
            pe.wait_ge(v_own_ready, 2)
            for p in range(2):
                for half in range(2):
                    pe.matmul(bank[2 * p + half], kd_tok[:, NTILE, 2 * p:2 * p + 2],
                              v_own[:, p, 4 * half:4 * half + 4], start=True, stop=True).then_inc(ret_kv, 1)
            pe.wait_ge(ret_o_evac, NT)
            for p in range(2):
                sums(Q_HEAD + 6 * p, bd, z[:, Z_RQ + p])
                pe.wait_ge(head_squared, p + 1)
                sums(Q_HEAD + 6 * p + 3, bd, square)
            def pass_projections(i):
                def queries(hh):
                    for c in range(NCH):
                        if hh == 1:
                            pe.wait_ge(q_evac, 6 * i + c + 1)
                        for kb in range(2):
                            mm = pe.matmul(bank[c][:, 0:CH], w_pass[:, (2 * hh + kb) * P:(2 * hh + kb + 1) * P],
                                           z[:, Z_CQ + kb, frames(c)], start=kb == 0, stop=kb == 1)
                        mm.then_inc(pass_done, 1)

                def keys(c):
                    if c:
                        pe.wait_ge(kv_evac, 6 * i + 1)
                    pe.matmul(bank[3], w_pass[:, 512:640], z[:, Z_CKV, 512 * c:512 * c + 512], start=True,
                              stop=True).then_inc(pass_done, 1)

                for hh in range(2):
                    queries(hh)
                    keys(hh)
                for c in range(2):
                    pe.wait_ge(q_evac, 6 * i + 4 + c)
                    for k in range(4):
                        mm = pe.matmul(bank[c][:, tile(k)], z[:, Z_CKV, tile(4 * c + k)], w_pass[:, 640:768],
                                       start=True, stop=True)
                    mm.then_inc(pass_done, 1)
                for hh in range(2):
                    pe.wait_ge(q_evac, 6 * i + 6) if hh == 0 else pe.wait_ge(kv_evac, 6 * i + 2)
                    pe.matmul(bank[2 + hh][:, 0:TS], w_pass[0:64, 768 + P * hh:896 + P * hh], q_pass[0:64, hh, TP:T],
                              start=True, stop=True).then_inc(pass_done, 1)
                pe.wait_ge(q_ready, 2 * i + 2)
                pe.wait_ge(kv_evac, 6 * i + 6)
                pe.wait_ge(sb_staged, 2 * i + 2)

            def transposed(g, ring, blocks, reused, src):
                if reused:
                    pe.wait_ge(pt_copied, g - 1)
                for b in range(blocks):
                    mm = pe.transpose(bank[4 + ring % 2][:, tile(b)], src[:, tile(b)], ident[:])
                mm.then_inc(pt_done, 1)

            pe.wait_ge(setup_done, 4)
            with pe.Fori(0, NP) as i:
                pe.wait_ge(w_pass_in, 16 * i + 16)
                pass_projections(i)
                for n in range(N_LOOP + 2):
                    if n < N_LOOP:
                        kind, j = KINDS[n]
                        width = P * j + P
                        if n >= 2:
                            k2, j2 = KINDS[n - 2]
                            if k2 < 2:
                                pe.wait_ge(exp_done, 16 * i + 2 * j2 + k2 + 1)
                            else:
                                pe.wait_ge(sb_arg, 8 * i + j2 + 1)
                        pe.wait_ge(kpe_ready, 1)
                        for at in range(0, width, 512):
                            w = min(512, width - at)
                            if kind < 2:
                                mm = pe.matmul(S[n % 2][:, at:at + w], q_pass[0:96, kind, tile(j)],
                                               k_pass[0:96, kind, at:at + w], start=True, stop=True)
                            else:
                                mm = pe.matmul(S[n % 2][:, at:at + w], sb_q[:, tile(j)],
                                               z[:, bass.ds(Z_SK + i, 1), at:at + w].rearrange("p a n -> p (a n)"),
                                               start=True, stop=True)
                        mm.then_inc(s_ready, 1)
                    if n >= 2:
                        kind, j = KINDS[n - 2]
                        groups = range(G_BEFORE[n - 2], G_BEFORE[n - 1])
                        if kind < 2:
                            pe.wait_ge(p_norm, 16 * i + 2 * j + kind + 1)
                        else:
                            pe.wait_ge(sb_p, 8 * i + j + 1)
                        for g in groups:
                            k0 = 4 * (g - groups[0])
                            transposed(G_PASS * i + g, g, min(4, j + 1 - k0), g >= 2, prob[:, kind, k0 * P:])
                        if n >= 4:
                            pe.wait_ge(o_evac, N_LOOP * i + n - 3)
                        rows = slice(64, P) if kind == 1 else slice(0, 64)
                        for g in groups:
                            pe.wait_ge(pt_copied, G_PASS * i + g + 1)
                            k0 = 4 * (g - groups[0])
                            for b in range(min(4, j + 1 - k0)):
                                v = v_pass[:, k0 + b, 64 * kind:64 * kind + 64] if kind < 2 else sv_pass[:, k0 + b]
                                mm = pe.matmul(bank[6 + n % 2][rows, 0:P], v, probT[:, g % 3, tile(b)],
                                               start=k0 + b == 0, stop=k0 + b == j)
                            mm.then_inc(pv_done, 1)
            pe.wait_ge(o_evac, T_MLA_S)
            pe.transpose(bank[4][:, 0:P], z[:, Z_CKV, TP:T], ident[:]).then_inc(new_done, 1)
            pe.wait_ge(new_ready, 1)
            for n in range(DB + 1):
                if n < DB:
                    if n >= 2:
                        pe.wait_ge(exp_done, 2 * NP * NTILE + n - 1)
                    pe.wait_ge(lat_in[n % 2], 48 * (n // 2 + 1))
                    for at, w, latent, rotary in ((0, PAST, lat[:, n % 2, 0], lat[64:96, n % 2, 1]),
                                                  (PAST, TS, z[:, Z_CKV, TP:T], z[64:96, Z_KPE, TP:T])):
                        own_s = S[n % 2][:, at:at + w]
                        pe.matmul(own_s, q_abs[:, n], latent, start=True, stop=False)
                        mm = pe.matmul(own_s, q_pe[:, n], rotary, start=False, stop=True)
                    mm.then_inc(s_ready, 1)
                if n >= 1:
                    b = n - 1
                    pe.wait_ge(p_norm, 2 * NP * NTILE + b + 1)
                    for g in range(2):
                        transposed(G_MLA_S + 2 * b + g, 2 * b + g, (4, 1)[g], True, prob[:, b % 3, 512 * g:])
                    pe.wait_ge(o_evac, T_MLA_S + max(0, b - 1))
                    for g in range(2):
                        pe.wait_ge(pt_copied, G_MLA_S + 2 * b + g + 1)
                        for k in range((4, 1)[g]):
                            v = lat[:, b % 2, 2, tile(k)] if g == 0 else ckv_new[:]
                            mm = pe.matmul(bank[6 + b % 2][:, 0:P], v, probT[:, (2 * b + g) % 3, tile(k)],
                                           start=g == 0 and k == 0, stop=g == 1)
                        mm.then_inc(pv_done, 1)
            pe.wait_ge(o_evac, T_SB_S)
            pe.wait_ge(sample_in, 64)
            for h in range(MH):
                mm = pe.matmul(bank[7][64 * (h % 2):64 * (h % 2) + 64, tile(h // 2)], w_v[:, VD * h:VD * h + VD],
                               o_lat[:, :, h], start=True, stop=True)
            mm.then_inc(o_heads, 1)
            pe.wait_ge(sk_new_ready, 1)
            for n in range(DB // 2 + 1):
                if n < DB // 2:
                    if n >= 2:
                        pe.wait_ge(sb_arg, NP * NTILE + n - 1)
                    pe.wait_ge(sb_pair_ready, n + 1)
                    pe.wait_ge(cache_in[n % 2], 32 * (n // 2 + 1))
                    for bb in range(2):
                        for f in range(2):
                            pe.matmul(S[n % 2][:, 0:PAST], sb_pair[:, n % 2, bb, f], cache_k[n % 2][:, bb, f],
                                      start=bb + f == 0, stop=bb + f == 2)
                    for bb in range(2):
                        for f in range(2):
                            mm = pe.matmul(S[n % 2][:, PAST:PAST + TS], sb_pair[:, n % 2, bb, f], sk_new[:, f],
                                           start=bb + f == 0, stop=bb + f == 2)
                    mm.then_inc(s_ready, 1)
                if n >= 1:
                    p = n - 1
                    pe.wait_ge(sb_p, NP * NTILE + p + 1)
                    for g in range(2):
                        transposed(G_SB_S + 2 * p + g, 1 + 2 * p + g, (4, 1)[g], True, prob[:, p % 3, 512 * g:])
                    pe.wait_ge(o_sample, 1)
                    pe.wait_ge(o_evac, T_SB_S + max(0, p - 1))
                    pe.wait_ge(pt_copied, G_SB_S + 2 * p + 2)
                    for bb in range(2):
                        for f in range(2):
                            out = bank[6 + p % 2][:, (2 * bb + f) * 64:(2 * bb + f) * 64 + 64]
                            for k in range(5):
                                v = (cache_v[p % 2][:, bb, k, tile(f)] if k < 4 else
                                     sv_tok[:, NTILE, 2 * f:2 * f + 2])
                                at = P * (k % 4) + 64 * bb
                                mm = pe.matmul(out, v, probT[:, (1 + 2 * p + k // 4) % 3, at:at + 64],
                                               start=k == 0, stop=k == 4)
                    mm.then_inc(pv_done, 2)

            pe.wait_ge(mix_split, KB)
            for m in range(KB):
                projection(m % 2, W_OUT + m, 3 * (NZ + m - 2), mix_hi, mix_lo)
            pe.wait_ge(x_split, 2 * KB)
            for m in range(GH):
                projection(m % 2, W_MQ + m, 3 * (NZ + KB + m - 2), act_hi, act_lo)
                if m == 0:
                    pe.wait_ge(x_summed, 2 * KB)
                    sums(Q_MQ, ones, sumsq)
            n_mem = NTILE + DB // 2
            pe.wait_ge(g_evac, G_MO)
            pe.wait_ge(qm_zero, 1)
            for n in range(n_mem + 1):
                if n < n_mem:
                    if n >= 2:
                        pe.wait_ge(m_exp, n - 1)
                    if n < NTILE:
                        for h in range(GH):
                            mm = pe.matmul(S[n % 2][:, MEM * h:MEM * h + MEM], qm[:, h, tile(n)], mkv[:, h],
                                           start=True, stop=True)
                    else:
                        p = n - NTILE
                        pe.wait_ge(qm_pair_ready, p + 1)
                        pe.wait_ge(m_cache_in[p % 2], 32 * (p // 2 + 1))
                        for bb in range(2):
                            for h in range(GH):
                                mm = pe.matmul(S[n % 2][:, 0:MEM], qm_pair[:, p % 2, bb, h], mk_c[:, p % 2, bb, h],
                                               start=bb + h == 0, stop=bb * 4 + h == 7)
                    mm.then_inc(ms_ready, 1)
                if n >= 1:
                    c = n - 1
                    pe.wait_ge(m_norm, c + 1)
                    blocks = 4 if c < NTILE else 1
                    for g in range(2):
                        if c >= 1:
                            pe.wait_ge(mt_copied, 2 * c - 1 + g)
                        for b in range(blocks):
                            mm = pe.transpose(bank[4 + g][:, tile(b)], m_prob[:, c % 2, tile(blocks * g + b)], ident[:])
                        mm.then_inc(mt_done, 1)
                    pe.wait_ge(mt_copied, 2 * c + 2)
                    if c >= 2:
                        pe.wait_ge(om_split, c - 1)
                    out = bank[6 + c % 2]
                    if c < NTILE:
                        for h in range(GH):
                            for k in range(2):
                                b = 2 * h + k
                                mm = pe.matmul(out[:, tile(h)], mem_v[:, k, tile(h)],
                                               m_probT[:, 2 * (c % 2) + b // 4, tile(b % 4)], start=k == 0, stop=k == 1)
                    else:
                        p = c - NTILE
                        for h in range(GH):
                            for bb in range(2):
                                for k in range(2):
                                    at = 64 * bb + DS * h
                                    mm = pe.matmul(out[:, 2 * DS * h + DS * bb:2 * DS * h + DS * bb + DS],
                                                   mv_c[:, p % 2, bb, k, tile(h)],
                                                   m_probT[:, 2 * (c % 2) + k, at:at + DS], start=k == 0, stop=k == 1)
                    mm.then_inc(m_pv, 1)
            pe.wait_ge(om_split, n_mem)
            for m in range(KB):
                k = (m // 2) % 2
                if m % 2 == 0:
                    pe.wait_ge(w_split, W_MO + m // 2 + 1)
                for c in range(NCH):
                    pe.wait_ge(g_evac, G_MO + 3 * (m - 2) + c + 1)
                    mm = split_products(bank[3 * (m % 2) + c][:, 0:CH], k, 4 * (m % 2), 4,
                                        lambda kb: om_hi[:, kb, frames(c)], lambda kb: om_lo[:, kb, frames(c)])
                    mm.then_inc(w_used if m % 2 and c == NCH - 1 else g_done, 1)
            pe.wait_ge(x_summed, 3 * KB)
            sums(Q_FFN, ones, sumsq)

            def down_projection(g, first_slot):
                pe.wait_ge(s_split, 2 * g + 2)
                for m in range(KB):
                    k = m // 4
                    if m % 4 == 0:
                        pe.wait_ge(w_split, first_slot + k + 1)
                    for c in range(NCH):
                        q = NCH * m + c
                        if q >= 2:
                            pe.wait_ge(d_evac, 3 * KB * g + q - 1)
                        split_products(bank[6 + q % 2][:, 0:CH], k, 2 * (m % 4), 2, lambda kb: s_hi[:, kb, frames(c)],
                                       lambda kb: s_lo[:, kb, frames(c)]).then_inc(w_used if q % 12 == 11 else d_done, 1)

            pe.wait_ge(x_split, 3 * KB)
            for u in range(4):
                projection(u % 2, W_FFN + u, G_UP + NCH * (u - 2), act_hi, act_lo)
            with pe.Fori(1, NGRP) as i:
                slot = 6 * i + (W_FFN - 2)
                for ab in range(2):
                    projection(ab, slot + ab, 12 * i + (G_UP + NCH * (ab - 2)), act_hi, act_lo)
                down_projection(i - 1, slot + 2)
                for ab in range(2):
                    projection(ab, slot + 4 + ab, 12 * i + (G_UP + NCH * ab), act_hi, act_lo)
            down_projection(NGRP - 1, NW - 2)
            pe.wait_ge(x_summed, 4 * KB)
            sums(Q_FINAL, ones, sumsq)



def rope_swap(n):
    return np.roll(np.arange(n), -(n // 2))


def feature_major(x):
    return np.ascontiguousarray(x.T.reshape(-1, P, x.shape[0]).transpose(1, 0, 2))


def column_blocks(w):
    k, m = w.shape
    return w.reshape(k // P, P, m // P, P).transpose(2, 1, 0, 3)


def pack_w_in(w):
    cq, ckv, kpe, rq, rk, rv, rg, sq, sk, sv = np.split(w, np.cumsum((QL, KVL, ROPE) + (RH * HD,) * 7)[:-1], axis=1)
    swapped = kpe[:, rope_swap(ROPE)]
    parts = [cq, ckv, kpe, swapped, kpe, swapped, rq, rk, rg]
    for h in range(SH):
        parts += [sq[:, h * HD:h * HD + HD], sv[:, h * HD:h * HD + HD]]
    for h in range(SH):
        parts += [sk[:, h * HD:h * HD + HD], rv[:, h * HD:h * HD + HD]]
    return np.concatenate(parts, axis=1)


def positions():
    return np.concatenate([np.arange(TP), np.tile(PAST + np.arange(DS), DB)]).astype(np.float64)


def layout(a):
    io = {}
    w_up, w_down = a["w_ffn_up"][0], a["w_ffn_down"][0]
    slots = [column_blocks(a["w_mem_k"][0]), column_blocks(a["w_mem_v"][0]), column_blocks(pack_w_in(a["w_in"][0]))]
    w_out = a["w_out"][0]
    rows = [w_out[:MH * VD]]
    for h in range(SH):
        rows += [w_out[MH * VD + RH * HD + h * HD:][:HD], w_out[MH * VD + h * HD:][:HD]]
    slots += [column_blocks(np.concatenate(rows)), column_blocks(a["w_mem_q"][0])]
    slots.append(column_blocks(a["w_mem_o"][0]).reshape(4, 2, P, 4, P).transpose(0, 2, 1, 3, 4))
    up = column_blocks(w_up)
    down = w_down.reshape(NGRP, 2, P, 2, 4, P).transpose(0, 3, 2, 4, 1, 5)
    slots = [s.reshape(-1, P, KB * P) for s in slots]
    for g in range(NGRP):
        slots.append(up[[2 * g, NFF + 2 * g]].reshape(-1, P, KB * P))
        if g:
            slots.append(down[g - 1].reshape(-1, P, KB * P))
        slots.append(up[[2 * g + 1, NFF + 2 * g + 1]].reshape(-1, P, KB * P))
    slots.append(down[NGRP - 1].reshape(-1, P, KB * P))
    io["wstream"] = np.concatenate(slots)
    x = np.concatenate([a["x_prompt"][0], a["x_sample"].reshape(TS, D)])
    io["xT"] = feature_major(x)
    io["mT"] = feature_major(a["mem_prompt"][0])

    gamma = 1.0 - 2.0 ** (-5.0 - np.arange(RH))
    pair = np.repeat(gamma.reshape(2, 2), HD, axis=1).T
    col = lambda g: g.reshape(-1, P).T
    parts = dict(g_mix=col(a["g_mix"][0]), g_mem_q=col(a["g_mem_q"][0]), g_mem_kv=col(a["g_mem_kv"][0]),
                 g_ffn=col(a["g_ffn"][0]), g_final=col(a["g_final"]), g_q=col(a["g_q_lora"][0]),
                 g_kv=col(a["g_kv_lora"][0]), g_ret=col(a["g_ret_norm"][0]),
                 decay128=(pair ** P).astype(np.float32), decay16=(pair ** DS).astype(np.float32),
                 b_conv=col(a["b_ffn_conv"][0]),
                 w_conv=a["w_ffn_conv"][0].reshape(3, 2 * NFF, P).transpose(2, 1, 0).reshape(P, -1))
    io["consts"] = np.concatenate([parts[n] for n, _ in CONSTS], axis=1).astype(np.float32)
    io["conv0"] = a["state_ffn_conv"][0].transpose(2, 0, 1).reshape(2 * NFF, P, 2 * DB).transpose(1, 0, 2)
    io["ident"] = np.eye(P, dtype=np.float32)
    io["bd"] = np.kron(np.eye(2), np.ones((HD, HD))) / HD
    pos = positions()
    inv = 10000.0 ** (-np.arange(0, HD, 2) / HD)
    ang = pos[None, :] * np.tile(inv, 4)[:, None]
    sign = np.tile(np.repeat([-1.0, 1.0], HD // 2), 2)[:, None]
    io["rope_ret"] = np.stack([np.cos(ang), sign * np.sin(ang)])
    inv = 10000.0 ** (-np.arange(0, ROPE, 2) / ROPE)
    ang = pos[None, :] * np.tile(inv, 2)[:, None]
    sign = np.repeat([-1.0, 1.0], ROPE // 2)[:, None]
    io["rope_pe"] = np.concatenate([np.ones((64, T)), np.cos(ang), sign * np.sin(ang)])
    r_ = np.arange(P)
    strictly = r_[None, :] < r_[:, None]
    io["before"] = np.stack([strictly * 1.0, np.where(strictly, 0.0, NEG)]).transpose(1, 0, 2)
    wq = a["w_q_up"][0].reshape(2, P, MH, NOPE + ROPE)
    wq = np.concatenate([wq, wq[..., NOPE + rope_swap(ROPE)]], axis=3)
    wkv = a["w_kv_up"][0].reshape(KVL, MH, NOPE + VD)
    w_pass = np.zeros((NP, P, 1024), np.float32)
    w_pass[:, :, 0:512] = wq.reshape(2, P, NP, 2, P).transpose(2, 1, 3, 0, 4).reshape(NP, P, 512)
    w_pass[:, :, 512:640] = wkv[:, :, :NOPE].reshape(P, NP, 2 * NOPE).transpose(1, 0, 2)
    w_pass[:, :, 640:768] = wkv[:, :, NOPE:].reshape(P, NP, 2 * VD).transpose(1, 0, 2)
    w_pass[:, :NOPE, 768:] = wkv[:, :, :NOPE].reshape(P, NP, 2, NOPE).transpose(1, 3, 2, 0).reshape(NP, NOPE, 2 * P)
    io["w_pass"] = w_pass
    lat = a["cache_mla_ckv"][0]
    io["lat"] = np.stack([lat.transpose(0, 2, 1), lat.reshape(DB, 4, P, KVL).transpose(0, 2, 1, 3).reshape(DB, P, PAST)], 1)
    io["kpe_c"] = a["cache_mla_kpe"][0].transpose(0, 2, 1)
    io["w_v"] = wkv[:, :, NOPE:].reshape(P, MH * VD)
    io["cache_k"] = a["cache_sb_k"][0].reshape(4, 2, PAST, 2, P).transpose(0, 4, 1, 3, 2)
    io["cache_v"] = a["cache_sb_v"][0].reshape(4, 2, 4, P, SH * HD).transpose(0, 3, 1, 2, 4)
    io["mk_c"] = a["cache_mem_k"][0].reshape(4, 2, MEM, GH, P).transpose(0, 4, 1, 3, 2)
    io["mv_c"] = a["cache_mem_v"][0].reshape(4, 2, 2, P, GH * P).transpose(0, 3, 1, 2, 4)
    col_ = np.arange(15 * DS)
    io["own_band"] = np.broadcast_to(np.where(col_ // DS == DB - 1, 0.0, NEG), (P, 15 * DS))
    col_ = np.arange(14 * DS)[None, :]
    row_ = np.arange(P)[:, None]
    keep = (col_ // DS == DB - 2 + row_ // 64) & (col_ % DS < row_ % DS)
    io["keep_band"] = keep * 1.0
    io["hide_band"] = np.where(keep, 0.0, NEG)
    i = np.arange(P)
    diff = i[None, :] - i[:, None]
    same = (i[None, :] // DS) == (i[:, None] // DS)
    power = gamma[:, None, None] ** np.maximum(diff, 0)
    io["ret_mask"] = np.stack([power * (diff >= 0), power * ((diff >= 0) & same)]).reshape(2, 2, 2, P, P).transpose(
        3, 0, 2, 1, 4).reshape(P, 2, 2, 2 * P)
    q_pow = np.stack([i + 1, i % DS + 1])
    io["q_decay"] = pair[:, None, :, None] ** q_pow[None, :, None, :]
    k_pow = np.stack([P - 1 - i, DS - 1 - i % DS])
    io["k_decay"] = np.broadcast_to((gamma[None, None, :] ** k_pow.T[:, :, None])[..., None], (P, 2, RH, HD))
    io["own"] = (i[:, None] // DS == np.arange(DB)[None, :]).astype(np.float64)
    s0 = np.zeros((2, HD, DB, 2, 2, HD), np.float32)
    st = a["state_ret"][0].reshape(DB, 2, 2, HD, HD)
    for hh in range(2):
        s0[hh, :, :, :, hh] = st[:, :, hh].transpose(2, 0, 1, 3)
    io["s0"] = s0.reshape(P, DB, 2, P)
    return io


OUTS = {"o_mkv": (P, 8, MEM), "o_skv": (P, 8, T), "o_ckv": (P, T), "o_kpe": (ROPE, T), "o_state": (P, 2, P), "o_s0": (P, DB, 2, P),
        "o_conv": (P, 2 * NFF, 2 + 2 * DB), "o_y": (P, KB, T)}


def kernel(**inputs):
    import concourse.bacc as bacc
    from concourse.bass_utils import run_bass_kernel_spmd

    nc = bacc.Bacc("TRN2", target_bir_lowering=False, num_devices=1)
    arrays = {k: np.ascontiguousarray(v, dtype=np.float32) for k, v in layout({k: np.asarray(v) for k, v in inputs.items()}).items()}
    io = {k: nc.dram_tensor(k, v.shape, F32, kind="ExternalInput").ap() for k, v in arrays.items()}
    for name, shape in OUTS.items():
        io[name] = nc.dram_tensor(name, shape, F32, kind="ExternalOutput").ap()
    io["x_mid"] = nc.dram_tensor("x_mid", (P, KB, T), F32, kind="Internal").ap()
    build(nc, io)
    r = run_bass_kernel_spmd(nc, [arrays], core_ids=[0]).results[0]
    return assemble(r)


def assemble(r):
    y = r["o_y"].transpose(2, 1, 0).reshape(T, D)
    mkv = r["o_mkv"].transpose(1, 2, 0)
    ckv, kpe = r["o_ckv"].T, r["o_kpe"].T
    qv, kv = r["o_skv"][:, :SH], r["o_skv"][:, SH:]
    sbk = kv[:HD].transpose(2, 1, 0)
    sbv = qv[HD:].transpose(2, 1, 0)
    pairs = range(2)
    state = r["o_state"].reshape(2, HD, 2, 2, HD)
    state = np.stack([state[hh, :, p, hh] for p in pairs for hh in pairs])
    s0 = r["o_s0"].reshape(2, HD, DB, 2, 2, HD)
    s0 = np.stack([s0[hh, :, :, p, hh].transpose(1, 0, 2) for p in pairs for hh in pairs], axis=1)
    conv = r["o_conv"].transpose(2, 1, 0).reshape(2 + 2 * DB, 2 * DFF)
    sample = lambda v: v[TP:].reshape((1, DB, DS) + v.shape[1:])
    prompt = lambda v: v[:TP][None, None]
    out = (y[:TP][None], y[TP:].reshape(DB, DS, D), prompt(ckv), prompt(kpe), state[None, None], prompt(sbk), prompt(sbv),
           mkv[:GH].transpose(1, 0, 2)[None, None], mkv[GH:].transpose(1, 0, 2)[None, None], conv[:2][None, None],
           sample(ckv), sample(kpe), s0[None], sample(sbk), sample(sbv), conv[2:].reshape(1, DB, 2, 2 * DFF))
    return tuple(np.ascontiguousarray(v) for v in out)
```
